# Optimizing a Trainium2 kernel written in Bass

```python
import math
import jax, jax.numpy as jnp
from jax import lax
import numpy as np

D_MODEL = 1024
BATCH = 1
SEQ = 1024
DEPTH = 1

CHUNK = 64
HEAD_DIM = 64
A_HEADS = 8
A_KV_HEADS = 2
A_GROUP = A_HEADS // A_KV_HEADS
A_WINDOW = 128
A_WINDOW_CHUNKS = A_WINDOW // CHUNK
B_HEADS = 4
Q_BLOCK = 128
C_WIDTH = 512
CONV_WIDTH = 3
D_FF = -(-8 * D_MODEL // (3 * 256)) * 256
A_WIDTH = A_HEADS * HEAD_DIM
B_WIDTH = B_HEADS * 2 * HEAD_DIM
N_BRANCH = 3
SPLIT_SIZES = (A_HEADS * HEAD_DIM, A_KV_HEADS * HEAD_DIM, A_KV_HEADS * HEAD_DIM,
               B_HEADS * 2 * HEAD_DIM, B_HEADS * 2 * HEAD_DIM, B_HEADS * 2 * HEAD_DIM,
               C_WIDTH, C_WIDTH, C_WIDTH)
SPLIT_POINTS = tuple(int(v) for v in np.cumsum(SPLIT_SIZES)[:-1])
IN_WIDTH = sum(SPLIT_SIZES)
ALPHA = (2 * DEPTH) ** 0.25
BETA = (8 * DEPTH) ** -0.25
NEG = -1e30
EPS = 1e-5

kernel_name = 'hybrid_chunk_causal_encoder'

def alibi_slopes(n):
    return jnp.exp2(-8.0 * jnp.arange(1, n + 1, dtype=jnp.float32) / n)

def layer_norm(x, g, b):
    xf = x.astype(jnp.float32)
    mu = jnp.mean(xf, axis=-1, keepdims=True)
    var = jnp.mean(jnp.square(xf - mu), axis=-1, keepdims=True)
    return ((xf - mu) * lax.rsqrt(var + EPS)).astype(x.dtype) * g + b

def rms_norm(x, g):
    xf = x.astype(jnp.float32)
    return (xf * lax.rsqrt(jnp.mean(jnp.square(xf), axis=-1, keepdims=True) + EPS)).astype(x.dtype) * g

def shift_chunks(z, n):
    if n == 0:
        return z
    return jnp.concatenate([jnp.zeros_like(z[:, :n]), z[:, :-n]], axis=1)

def window_sink_attention(q, k, v, sink):
    bsz, s_len, _ = q.shape
    n_chunks = s_len // CHUNK
    w = A_WINDOW_CHUNKS
    qc = q.reshape(bsz, n_chunks, CHUNK, A_KV_HEADS, A_GROUP, HEAD_DIM)
    kc = k.reshape(bsz, n_chunks, CHUNK, A_KV_HEADS, HEAD_DIM)
    vc = v.reshape(bsz, n_chunks, CHUNK, A_KV_HEADS, HEAD_DIM)
    kb = jnp.concatenate([shift_chunks(kc, w - 1 - i) for i in range(w)], axis=2)
    vb = jnp.concatenate([shift_chunks(vc, w - 1 - i) for i in range(w)], axis=2)
    logits = jnp.einsum('bcqkgd,bcjkd->bckgqj', qc, kb).astype(jnp.float32) * (HEAD_DIM ** -0.5)
    qpos = jnp.arange(CHUNK)
    jpos = jnp.arange(w * CHUNK)
    dist = jnp.abs(qpos[:, None] + (w - 1) * CHUNK - jpos[None, :]).astype(jnp.float32)
    slopes = alibi_slopes(A_HEADS).reshape(A_KV_HEADS, A_GROUP)
    logits = logits - slopes[:, :, None, None] * dist
    key_chunk = jnp.arange(n_chunks)[:, None] - (w - 1) + jpos[None, :] // CHUNK
    valid = key_chunk >= 0
    logits = jnp.where(valid[None, :, None, None, None, :], logits, NEG)
    sink_l = jnp.broadcast_to(sink.astype(jnp.float32).reshape(A_KV_HEADS, A_GROUP)[None, None, :, :, None, None],
                              logits.shape[:-1] + (1,))
    probs = jax.nn.softmax(jnp.concatenate([logits, sink_l], axis=-1), axis=-1)[..., :-1]
    out = jnp.einsum('bckgqj,bcjkd->bcqkgd', probs.astype(v.dtype), vb)
    return out.reshape(bsz, s_len, A_WIDTH)

def differential_attention(q, k, v, lam, subln_g, lambda_init):
    bsz, s_len, _ = q.shape
    n_qb = s_len // Q_BLOCK
    q = q.reshape(bsz, s_len, B_HEADS, 2, HEAD_DIM)
    k = k.reshape(bsz, s_len, B_HEADS, 2, HEAD_DIM)
    v = v.reshape(bsz, s_len, B_HEADS, 2 * HEAD_DIM)
    qb = jnp.moveaxis(q.reshape(bsz, n_qb, Q_BLOCK, B_HEADS, 2, HEAD_DIM), 1, 0)
    slopes = alibi_slopes(B_HEADS)
    kpos = jnp.arange(s_len)

    def block(args):
        qblk, i = args
        tpos = i * Q_BLOCK + jnp.arange(Q_BLOCK)
        logits = jnp.einsum('bqhmd,bkhmd->bhmqk', qblk, k).astype(jnp.float32) * (HEAD_DIM ** -0.5)
        dist = jnp.abs(tpos[:, None] - kpos[None, :]).astype(jnp.float32)
        logits = logits - slopes[:, None, None, None] * dist
        visible = kpos[None, :] < (tpos[:, None] // CHUNK + 1) * CHUNK
        logits = jnp.where(visible, logits, NEG)
        p = jax.nn.softmax(logits, axis=-1)
        wgt = p[:, :, 0] - lam * p[:, :, 1]
        return jnp.einsum('bhqk,bkhe->bqhe', wgt.astype(v.dtype), v)

    o = lax.map(block, (qb, jnp.arange(n_qb)))
    o = jnp.moveaxis(o, 0, 1).reshape(bsz, s_len, B_HEADS, 2 * HEAD_DIM)
    o = rms_norm(o, subln_g) * (1.0 - lambda_init)
    return o.reshape(bsz, s_len, B_WIDTH)

def short_gated_conv(b_gate, c_gate, u, conv_w):
    z = c_gate * u
    z = lax.conv_general_dilated(z, conv_w[:, None, :].astype(z.dtype), window_strides=(1,),
                                 padding=[(CONV_WIDTH - 1, 0)],
                                 dimension_numbers=('NWC', 'WIO', 'NWC'),
                                 feature_group_count=C_WIDTH)
    return b_gate * z

def setup_inputs(seed: int = 0) -> dict:
    key = jax.random.key(seed)
    ks = jax.random.split(key, 20)
    f32 = jnp.float32
    nrm = lambda k, shape, scale: jax.random.normal(k, shape, f32) * scale
    return {
        'x': nrm(ks[0], (BATCH, SEQ, D_MODEL), 1.0),
        'w_in': nrm(ks[1], (DEPTH, D_MODEL, IN_WIDTH), D_MODEL ** -0.5),
        'sink': nrm(ks[2], (DEPTH, A_HEADS), 0.5),
        'lam_q1': nrm(ks[3], (DEPTH, HEAD_DIM), 0.1),
        'lam_k1': nrm(ks[4], (DEPTH, HEAD_DIM), 0.1),
        'lam_q2': nrm(ks[5], (DEPTH, HEAD_DIM), 0.1),
        'lam_k2': nrm(ks[6], (DEPTH, HEAD_DIM), 0.1),
        'subln_g': 1.0 + nrm(ks[7], (DEPTH, 2 * HEAD_DIM), 0.02),
        'conv_w': nrm(ks[8], (DEPTH, CONV_WIDTH, C_WIDTH), CONV_WIDTH ** -0.5),
        'w_branch': nrm(ks[9], (DEPTH, N_BRANCH, A_WIDTH, D_MODEL), BETA * A_WIDTH ** -0.5),
        'w_gate': nrm(ks[10], (DEPTH, D_MODEL, N_BRANCH * D_MODEL), D_MODEL ** -0.5),
        'b_gate': nrm(ks[11], (DEPTH, N_BRANCH * D_MODEL), 0.01),
        'w_out': nrm(ks[12], (DEPTH, D_MODEL, D_MODEL), BETA * D_MODEL ** -0.5),
        'ln1_g': 1.0 + nrm(ks[13], (DEPTH, D_MODEL), 0.02),
        'ln1_b': nrm(ks[14], (DEPTH, D_MODEL), 0.01),
        'w_ffn_in': nrm(ks[15], (DEPTH, D_MODEL, 2 * D_FF), D_MODEL ** -0.5),
        'w_ffn_down': nrm(ks[16], (DEPTH, D_FF, D_MODEL), BETA * D_FF ** -0.5),
        'ln2_g': 1.0 + nrm(ks[17], (DEPTH, D_MODEL), 0.02),
        'ln2_b': nrm(ks[18], (DEPTH, D_MODEL), 0.01),
    }

def reference(x, w_in, sink, lam_q1, lam_k1, lam_q2, lam_k2, subln_g, conv_w, w_branch, w_gate, b_gate,
              w_out, ln1_g, ln1_b, w_ffn_in, w_ffn_down, ln2_g, ln2_b):
    bsz, s_len, _ = x.shape
    for l in range(DEPTH):
        proj = x @ w_in[l]
        qa, ka, va, qb, kb, vb, cb, cc, cu = jnp.split(proj, SPLIT_POINTS, axis=-1)
        y_a = window_sink_attention(qa, ka, va, sink[l])
        lambda_init = 0.8 - 0.6 * math.exp(-0.3 * l)
        lam = (jnp.exp(jnp.sum(lam_q1[l].astype(jnp.float32) * lam_k1[l].astype(jnp.float32)))
               - jnp.exp(jnp.sum(lam_q2[l].astype(jnp.float32) * lam_k2[l].astype(jnp.float32)))
               + lambda_init)
        y_b = differential_attention(qb, kb, vb, lam, subln_g[l], lambda_init)
        y_c = short_gated_conv(cb, cc, cu, conv_w[l])
        gates = jax.nn.sigmoid(x @ w_gate[l] + b_gate[l]).reshape(bsz, s_len, N_BRANCH, D_MODEL)
        merged = (gates[:, :, 0] * (y_a @ w_branch[l, 0])
                  + gates[:, :, 1] * (y_b @ w_branch[l, 1])
                  + gates[:, :, 2] * (y_c @ w_branch[l, 2]))
        x = layer_norm(ALPHA * x + merged @ w_out[l], ln1_g[l], ln1_b[l])
        gate, up = jnp.split(x @ w_ffn_in[l], 2, axis=-1)
        x = layer_norm(ALPHA * x + (jax.nn.silu(gate) * up) @ w_ffn_down[l], ln2_g[l], ln2_b[l])
    return x


_drawn_inputs = setup_inputs


def setup_inputs(seed=0):
    import zlib

    import numpy as np

    out = dict(_drawn_inputs(seed))
    spreads = {}
    factors = {'sink': 200.0,
     'lam_q1': 8.0,
     'lam_k1': 8.0,
     'lam_q2': 200.0,
     'lam_k2': 5.06,
     'subln_g': 28.799,
     'b_gate': 8.0,
     'ln1_b': 5.487,
     'ln2_g': 23.878,
     'ln2_b': 48.138}
    for name, (base, spread) in spreads.items():
        noise = np.random.default_rng([zlib.crc32(name.encode()), seed]).standard_normal(out[name].shape)
        drawn = base * np.exp(spread * noise) if base else spread * noise
        out[name] = __import__('jax').numpy.asarray(drawn.astype(out[name].dtype))
    for name, factor in factors.items():
        out[name] = (out[name] * factor).astype(out[name].dtype)
    return out
```

```python
import math

import concourse.bass as bass
from concourse import mybir
from concourse.alu_op_type import AluOpType as ALU
from contextlib import ExitStack

F32 = mybir.dt.float32
F32R = mybir.dt.float32r
BF16 = mybir.dt.bfloat16
ACT = mybir.ActivationFunctionType

PART = 128
HALF = 512
TOKENS = 1024
WIDTH = 1024
KT = WIDTH // PART
TILES = TOKENS // PART
CHUNK = 64
HEAD = 64
A_HEADS = 8
A_GROUP = 4
B_HEADS = 4
C_TILES = 4
BRANCH_KT = 4
WINDOW = 192
D_FF = 2816
FF_PAIRS = D_FF // PART
FF_TRIPS = FF_PAIRS // 2
ALPHA = 2.0 ** 0.25
EPS = 1e-5
LAMBDA_INIT = 0.8 - 0.6 * math.exp(-0.3 * 0)
Q_SCALE = -(HEAD ** -0.5)
RMS_SHIFT = 2.0 ** -20
MASKED = 1e32

COL_QB = (A_HEADS + 4) * HEAD
COL_KB = COL_QB + B_HEADS * PART
COL_VB = COL_KB + B_HEADS * PART
COL_CB = COL_VB + B_HEADS * PART
COL_CC = COL_CB + C_TILES * PART
COL_CU = COL_CC + C_TILES * PART
A_UNITS = COL_QB // PART

SCORES = (4, 5)
TURN = 6
VALUE = 7

AHEAD = 256
BUFFERS = 2


class Stage:

    def __init__(self, start, labels, trips=1):
        self.start, self.labels, self.trips = start, labels, trips
        self.place = {label: n for n, label in enumerate(labels)}
        assert len(self.place) == len(labels)
        self.said = 0

    @property
    def end(self):
        return self.start + len(self.labels) * self.trips

    def at(self, label, trip=0, back=0):
        n = self.start + self.place[label] + 1 - back * len(self.labels)
        return trip * len(self.labels) + n

    def step(self, label):
        assert self.labels[self.said % len(self.labels)] == label, (label, self.labels[self.said % len(self.labels)])
        self.said += 1
        return 1


def heads_script():
    atoms = [(0, [("decay",)]), (24 * 5, [("scores", 0, 0)]), (48 * 3 + 8, [("vturn", 0), ("vturn", 1)])]
    atoms += [(48 * 3 + 8, [("scores", 1, 0), ("mix", 0)]), (48 * 3 + 14, [("turn", 0, 0)])]
    slots = []
    for i in range(2, 8):
        slots.append([("scores", i, 0), ("mix", i - 1)])
        slots.append([("value", i - 2)] + ([("scores", i, 1)] if i >= 4 else []))
        slots.append([("turn", i - 1, 0)])
        if i - 1 >= 4:
            slots.append([("turn", i - 1, 1)])
    slots += [[("mix", 7)], [("value", 6)], [("turn", 7, 0)], [("turn", 7, 1)], [("value", 7)], [("rms",)]]
    first, last = 48 * 3 + 20, 48 * 6 - 12
    for n, slot in enumerate(slots):
        atoms.append((first + (last - first) * n // len(slots), slot))
    atoms.append((last, [("yturn", 0), ("yturn", 1)]))
    script, at = [], 0

    def dense(upto):
        nonlocal at
        while at < upto:
            n, a = divmod(at, 48)
            if a == 0:
                script.append(("split", n + 1))
            b = min(upto - 48 * n, 24 if a < 24 else 48)
            script.append(("mm", n, a, b))
            if b in (24, 48):
                script.append(("out", n, b // 24 - 1))
                if (n, b) == (4, 48):
                    script.append(("conv",))
            at = 48 * n + b

    for upto, steps in atoms:
        dense(upto)
        script.extend(steps)
    dense(48 * 6)
    return script


def heads_labels(script):
    vec, sca, ten = [], [], []
    for s in script:
        k, a = s[0], s[1:]
        if k == "decay":
            vec.append(s)
        elif k == "mm" and a[2] == 24:
            ten.append(("half", a[0]))
        elif k == "out":
            if a[0] in (0, 1, 2, 3, 5):
                sca.append(s)
            if a[0] == 5:
                vec.append(("gate", a[1]))
            if a[0] in (0, 1, 4, 5):
                vec.append(s)
        elif k == "conv":
            vec += [("conv", n) for n in range(3)]
        elif k == "scores":
            ten.append(s)
            vec += [("logit", *a, 0), ("logit", *a, 1)]
            if a[1] == 1:
                vec.append(("peak", a[0]))
            if a[1] == (a[0] >= 4):
                sca += [("exp", a[0], 0), ("exp", a[0], 1)]
        elif k == "mix":
            vec += [("inv", *a), ("norm", *a), ("lam", *a), ("mix", *a)]
        elif k in ("turn", "vturn", "yturn"):
            ten.append(s)
            sca.append(s)
            vec.append(s)
        elif k == "value":
            ten.append(s)
            sca.append(("tail", *a))
            vec += [("sum", *a), ("sq", *a)]
        elif k == "rms":
            sca.append(("root",))
            vec += [("rinv",), ("rscale",), ("rmul",)]
    return vec, sca, ten


def window_script():
    atoms = [(0, [("ksplit",), ("qsplit", 0)]), (10, [("vturn",)]), (18, [("scores", 0)]),
             (26, [("qsplit", 1)]), (34, [("scores", 1)]), (46, [("turn", 0, 0)]), (56, [("value", 0, 0)]),
             (60, [("turn", 0, 1)]), (70, [("value", 0, 1), ("norm", 0)]), (74, [("turn", 1, 0)]), (80, [("yturn", 0)]),
             (84, [("value", 1, 0)]), (88, [("turn", 1, 1)]), (98, [("value", 1, 1), ("norm", 1)]),
             (110, [("yturn", 1)]), (124, [("unmask",)])]
    script = []
    for e in range(2):
        at = 0

        def dense(upto):
            nonlocal at
            while at < upto:
                n, a = divmod(at, 48)
                if a == 0:
                    script.append(("split", 3 * e + n + 1))
                step = 24 if n < 2 else 12
                b = min(upto - 48 * n, (a // step + 1) * step)
                script.append(("mm", e, n, a, b))
                if b % step == 0:
                    script.append(("out", e, n, b // step - 1))
                at = 48 * n + b

        for upto, steps in atoms:
            dense(upto)
            script.extend((s[0], e, *s[1:]) for s in steps)
        dense(48 * 3)
        script += [("add", e), ("store", e)]
    return script


def window_labels(script):
    vec, sca, ten = [], [], []
    for s in script:
        k, a = s[0], s[1:]
        if k == "mm" and ((a[1] < 2 and a[3] == 24) or (a[1] == 2 and a[3] in (12, 24, 36))):
            ten.append(("part", a[0], a[1], a[3]))
        elif k == "out":
            (sca if a[1] < 2 else vec).append(s)
        elif k in ("ksplit", "qsplit"):
            sca.append(s)
            vec.append(s)
        elif k in ("turn", "vturn", "yturn"):
            ten.append(s)
            sca.append(s)
            vec.append(s)
        elif k == "scores":
            ten.append(s)
            vec += [("logit", *a, n) for n in range(A_GROUP)]
            sca += [("exp", *a, n) for n in range(A_GROUP)]
            vec.append(("sub", *a))
            sca.append(("sink", *a))
        elif k == "value":
            ten.append(s)
        elif k == "norm":
            sca.append(("tail", *a))
            vec += [("den", *a), ("inv", *a), ("sum", *a), ("norm", *a)]
        elif k in ("unmask", "add"):
            vec.append(s)
    return vec, sca, ten


def hybrid_encoder_layer(nc, x, w_in, sink, lam_q1, lam_k1, lam_q2, lam_k2, subln_g, conv_w, w_branch, w_gate,
                         b_gate, w_out, ln1_g, ln1_b, w_ffn_in, w_ffn_down, ln2_g, ln2_b, out):
    x_tiles = x[0].rearrange("(t p) d -> t p d", p=PART)
    out_tiles = out[0].rearrange("(t p) d -> t p d", p=PART)
    w_in_k = w_in[0].rearrange("(k p) c -> p k c", p=PART)
    w_gate_k = w_gate[0].rearrange("(k p) c -> p k c", p=PART)
    w_branch_k = w_branch[0].rearrange("n (k p) c -> p (n k) c", p=PART)
    w_out_k = w_out[0].rearrange("(k p) c -> p k c", p=PART)
    w_ffn_k = w_ffn_in[0].rearrange("(k p) c -> p k c", p=PART)
    w_down_k = w_ffn_down[0].rearrange("(k p) c -> k p c", p=PART)

    window_proj = nc.dram_tensor("window_proj", [A_UNITS, PART, PART + TOKENS], F32).ap()
    merged_bc = nc.dram_tensor("merged_bc", [KT, PART, TOKENS], F32).ap()

    ctx = ExitStack()
    with ctx:
        place = [1152]

        def put(name, shape, dt=F32, at=None):
            size = 2 if dt == BF16 else 4
            for n in shape[1:]:
                size *= n
            where = place[0] if at is None else at[0]
            t = nc.alloc_sbuf_tensor_at(name, shape, dt, offset=where)
            assert where + size <= 229344, (name, where + size)
            where = (where + size + 31) // 32 * 32
            if at is None:
                place[0] = where
            else:
                at[0] = where
            return t

        def sem(name):
            return ctx.enter_context(nc.semaphore(name))

        act_h = put("act_h", [PART, KT, TOKENS], F32R)
        act_l = put("act_l", [PART, KT, TOKENS], F32R)
        raw = [put(f"raw{n}", [PART, KT, PART]) for n in range(BUFFERS)]
        w_h = [put(f"w_h{n}", [PART, KT, PART], F32R) for n in range(BUFFERS)]
        w_l = [put(f"w_l{n}", [PART, KT, PART], F32R) for n in range(BUFFERS)]
        ident = put("ident", [PART, PART])
        gate_bias = put("gate_bias", [PART, 3 * KT])
        conv_taps = put("conv_taps", [PART, C_TILES, 3])
        rms_gain = put("rms_gain", [PART, 1])
        neg_sink = put("neg_sink", [PART, A_HEADS])
        neg_lam = put("neg_lam", [PART, 1])
        rms_eps = put("rms_eps", [PART, 1])
        ln_eps = put("ln_eps", [PART, 1])
        low = put("low", [PART, 2, 2, 2])
        den = put("den", [PART, 2, 2])
        inv = put("inv", [PART, 2, 2])
        square_sum = put("square_sum", [PART, TILES])
        rms_root = put("rms_root", [PART, TILES])
        rms_inv = put("rms_inv", [PART, TILES])
        a_low = put("a_low", [PART, A_HEADS])
        a_den = put("a_den", [PART, A_HEADS])
        a_sink = put("a_sink", [PART, A_HEADS])
        a_sunk = put("a_sunk", [PART, A_HEADS])
        a_inv = put("a_inv", [PART, A_HEADS])
        stats = put("stats", [PART, 2, 6])
        moments = put("moments", [PART, 2])
        ln_root = put("ln_root", [PART, 1])
        ln_inv = put("ln_inv", [PART, 1])
        base = place[0]
        KB = 1024

        at = [base]
        yb_h = put("yb_h", [PART, B_HEADS, TOKENS], F32R, at)
        yb_l = put("yb_l", [PART, B_HEADS, TOKENS], F32R, at)
        yc_h = put("yc_h", [PART, C_TILES, TOKENS], F32R, at)
        yc_l = put("yc_l", [PART, C_TILES, TOKENS], F32R, at)
        behind_y = at[0]
        q_h = put("q_h", [PART, TOKENS], F32R, at)
        q_l = put("q_l", [PART, TOKENS], F32R, at)
        k_h = put("k_h", [PART, TOKENS], F32R, at)
        k_l = put("k_l", [PART, TOKENS], F32R, at)
        v_hl = put("v_hl", [PART, TILES, 2 * PART], F32R, at)
        prob = [[put(f"prob{n}{m}", [PART, TOKENS], F32, at) for m in range(2)] for n in range(2)]
        bias_b = put("bias_b", [PART, TOKENS], F32, at)
        wt_h = put("wt_h", [PART, TILES, PART], F32R, at)
        wt_l = put("wt_l", [PART, TILES, PART], F32R, at)
        mixed = put("mixed", [PART, TILES, PART], F32, at)
        v_t = put("v_t", [PART, TOKENS], F32, at)
        conv = put("conv", [PART, TOKENS], F32, at)
        gated = put("gated", [PART, 2 + TOKENS], F32, at)
        o_tail = put("o_tail", [PART, PART], F32, at)
        at = [base]
        x_in = [put(f"x_in{n}", [PART, WIDTH], F32, at) for n in range(4)]
        lam_in = put("lam_in", [PART, 4, HEAD], F32, at)
        lam_out = put("lam_out", [PART, 2, HEAD], F32, at)
        lam_sum = put("lam_sum", [PART, 2], F32, at)
        lam_exp = put("lam_exp", [PART, 2], F32, at)
        sink_in = put("sink_in", [PART, A_HEADS], F32, at)
        gain_in = put("gain_in", [PART, 1], F32, at)
        zeros = put("zeros", [PART, PART], F32, at)
        ramp_b = put("ramp_b", [PART, TOKENS], F32, at)
        at = [behind_y]
        ya_h = put("ya_h", [PART, BRANCH_KT, TOKENS], F32R, at)
        ya_l = put("ya_l", [PART, BRANCH_KT, TOKENS], F32R, at)
        behind_ya = at[0]
        at = [behind_y]
        to_dram = [put(f"to_dram{n}", [PART, TOKENS], F32, at) for n in range(2)]
        ramp_a = put("ramp_a", [PART, WINDOW], F32, at)
        ramp_abs = put("ramp_abs", [PART, WINDOW], F32, at)
        at = [behind_ya]
        bias_a = put("bias_a", [PART, A_HEADS, WINDOW], BF16, at)
        near_a = put("near_a", [PART, A_HEADS, CHUNK], BF16, at)
        sig_b = put("sig_b", [PART, TOKENS], F32, at)
        sig_c = put("sig_c", [PART, TOKENS], F32, at)
        qf = put("qf", [PART, 4, PART], F32, at)
        kf = put("kf", [PART, 2, WINDOW], F32, at)
        vf = put("vf", [PART, 2 * PART], F32, at)
        qs_h = put("qs_h", [PART, 2, PART], F32R, at)
        qs_l = put("qs_l", [PART, 2, PART], F32R, at)
        ks_h = put("ks_h", [PART, 2, WINDOW], F32R, at)
        ks_l = put("ks_l", [PART, 2, WINDOW], F32R, at)
        vs_hl = put("vs_hl", [PART, 2, 2, 2 * HEAD], F32R, at)
        a_prob = [put(f"a_prob{g}", [PART, A_GROUP, 2 * PART], F32, at) for g in range(2)]
        at_h = put("at_h", [PART, 4, PART], F32R, at)
        at_l = put("at_l", [PART, 4, PART], F32R, at)
        a_tail = put("a_tail", [PART, A_GROUP, HEAD], F32, at)
        a_mix = put("a_mix", [PART, A_GROUP, HEAD], F32, at)
        at = [base]
        wo_h = put("wo_h", [PART, KT, WIDTH], F32R, at)
        wo_l = put("wo_l", [PART, KT, WIDTH], F32R, at)
        at = [behind_ya]
        merged = put("merged", [PART, TILES, WIDTH], F32, at)
        sig_a = put("sig_a", [PART, TOKENS], F32, at)
        at = [behind_y]
        m_h = [put(f"m_h{n}", [PART, KT, PART], F32R, at) for n in range(2)]
        m_l = [put(f"m_l{n}", [PART, KT, PART], F32R, at) for n in range(2)]
        normed = [put(f"normed{n}", [PART, WIDTH], F32, at) for n in range(2)]
        x_res = put("x_res", [PART, WIDTH], F32, at)
        ln_shift = put("ln_shift", [PART, WIDTH], F32, at)
        assert at[0] <= behind_ya
        at = [behind_ya + 32 * KB]
        ln_gain = put("ln_gain", [PART, WIDTH], F32, at)
        at = [base]
        h_h = [put(f"h_h{n}", [PART, TOKENS], F32R, at) for n in range(2)]
        h_l = [put(f"h_l{n}", [PART, TOKENS], F32R, at) for n in range(2)]
        wd_h = [put(f"wd_h{n}", [PART, WIDTH], F32R, at) for n in range(2)]
        wd_l = [put(f"wd_l{n}", [PART, WIDTH], F32R, at) for n in range(2)]
        silu = put("silu", [PART, TOKENS], F32, at)
        ln2_gain = put("ln2_gain", [PART, WIDTH], F32, at)
        ln2_shift = put("ln2_shift", [PART, WIDTH], F32, at)
        y_acc = merged

        bank = [ctx.enter_context(nc.psum_tensor(f"bank{n}", [PART, HALF], F32)) for n in range(8)]

        tensor_done = sem("tensor_done")
        vector_done = sem("vector_done")
        scalar_done = sem("scalar_done")
        units_done = sem("units_done")
        weights_hi = sem("weights_hi")
        weights_ready = sem("weights_ready")
        raw_landed = [sem(f"raw_landed{n}") for n in range(BUFFERS)]
        scores_seen = sem("scores_seen")
        moments_seen = sem("moments_seen")
        gates_seen = sem("gates_seen")
        queries_seen = sem("queries_seen")
        x_landed = [sem(f"x_landed{n}") for n in range(4)]
        small_landed = sem("small_landed")
        const_made = sem("const_made")
        zeros_stored = sem("zeros_stored")
        proj_stored = [sem(f"proj_stored{n}") for n in range(2)]
        bias_a_made = sem("bias_a_made")
        window_landed = sem("window_landed")
        merged_stored = sem("merged_stored")
        merged_landed = [sem(f"merged_landed{n}") for n in range(2)]
        ln_landed = sem("ln_landed")
        ln2_landed = sem("ln2_landed")
        res_landed = sem("res_landed")
        out_stored = sem("out_stored")

        X_TRIPS, X_PER = 2, 4
        x_labels = [("x", j, hh) for j in range(X_PER) for hh in range(2)]
        HEADS = heads_script()
        hv, hs, ht = heads_labels(HEADS)
        WIN = window_script()
        wv, ws, wt = window_labels(WIN)
        merge_v = [(k, e, h) for e in range(2) for h in range(2) for k in ("mul", "acc")]
        merge_s = [("out", e, h) for e in range(2) for h in range(2)]
        merge_t = [("part", e, n) for e in range(2) for n in range(2)]
        ln_v = ["st0", "st1", "ag", "ri", "z", "g", "b"]
        res_v = [(k, e) for e in range(2) for k in ["r0", "r1", "ms", *ln_v, "turn0", "turn1"]]
        res_s = [(k, e) for e in range(2) for k in ("ms", "root", "keep", "turn0", "turn1")]
        res_t = [(k, e) for e in range(2) for k in ("m0", "m1", "turn0", "turn1")]
        last_v = [(k, n) for n in (0, "t") for k in ["r0", "r1", *ln_v, "turn0", "turn1"]]
        last_s = [(k, n) for n in (0, "t") for k in ("root", "keep", "turn0", "turn1")]
        last_t = [("m0", 0), ("m1", 0)] + [(k, n) for n in (0, "t") for k in ("turn0", "turn1")]
        ff_v = [(k, s, h) for s in range(2) for h in range(2) for k in ("up", "lo")]
        ff_v += [("acc", t, h) for t in range(TILES) for h in range(2)]
        ff_s = [x for s in range(2) for x in (("silu", s, 0), ("silu", s, 1), ("hi", s, 0), ("hi", s, 1))]
        ff_t = [("half", n) for n in range(4)] + [("down", t, h) for t in range(TILES) for h in range(2)]
        end_v = [(k, t) for t in range(TILES) for k in ln_v]
        end_s = [("root", t) for t in range(TILES)]

        def chain(parts):
            stages, start = {}, AHEAD
            for name, labels, trips in parts:
                stages[name] = Stage(start, labels, trips)
                start = stages[name].end
            return stages

        init_v = ["l0", "l1", "dl", "nl", "gain", "sink", "ramp"]
        V = chain([("x", x_labels, X_TRIPS), ("init", init_v, 1), ("heads", hv, B_HEADS), ("window", wv, TILES // 2),
                   ("merge", merge_v, KT // 2), ("res0", ["ms0", "ms1"], 1), ("res", res_v, 3),
                   ("res7", last_v, 1), ("ff", ff_v, FF_TRIPS), ("end", end_v, 1)])
        S = chain([("x", x_labels, X_TRIPS), ("init", ["le"], 1), ("heads", hs, B_HEADS),
                   ("proj", [("out", e, h) for e in range(2) for h in range(2)], A_UNITS // 2),
                   ("window", ws, TILES // 2), ("merge", merge_s, KT // 2), ("res0", ["ms0", "ms1"], 1),
                   ("res", res_s, 3), ("res7", last_s, 1), ("ff", ff_s, FF_TRIPS), ("end", end_s, 1)])
        T = chain([("x", x_labels, X_TRIPS), ("heads", ht, B_HEADS),
                   ("proj", [("half", e) for e in range(2)], A_UNITS // 2), ("window", wt, TILES // 2),
                   ("merge", merge_t, KT // 2), ("res0", ["m0", "m1"], 1), ("res", res_t, 3), ("res7", last_t, 1),
                   ("ff", ff_t, FF_TRIPS)])

        ITEMS = {"heads": 0, "proj": 24, "window": 30, "merge": 54, "ff": 78}
        UNITS = {"heads": 0, "proj": 24, "window": 30, "merge": 54, "ff": 70}

        def item(stage, trip, n):
            per = {"heads": 6, "proj": 2, "window": 6, "merge": 6, "ff": 6}[stage]
            return trip * per + (ITEMS[stage] + n)

        def landed(stage, trip, n):
            per = {"heads": 6, "proj": 2, "window": 6, "merge": 6, "ff": 6}[stage]
            return trip * (8 * per) + 16 * ((ITEMS[stage] + n) // 2 + 1)

        def unit(stage, trip, n):
            per = {"heads": 6, "proj": 2, "window": 6, "merge": 4, "ff": 4}[stage]
            return trip * per + (UNITS[stage] + n)

        block = ctx.enter_context(nc.Block())

        @block.sync
        def _(sp):
            def load_item(stage, trip, n, src, kts=KT):
                sp.wait_ge(weights_ready, item(stage, trip, n) + 1)
                dst = raw[n % 2][:, 0:kts, :]
                sp.dma_start(dst, src).then_inc(raw_landed[n % 2], 16)

            for t in range(2):
                sp.dma_start(x_in[t][:, :], x_tiles[t]).then_inc(x_landed[t], 16)
            vectors = [(lam_in[:, n, :], v[0:1, :].partition_broadcast(PART))
                       for n, v in enumerate((lam_q1, lam_k1, lam_q2, lam_k2))]
            for dst, src in vectors:
                sp.dma_start(dst, src).then_inc(small_landed, 16)
            sp.dma_start(sink_in[:, :], sink[0:1, :].partition_broadcast(PART)).then_inc(small_landed, 16)
            for t in range(2, 4):
                sp.dma_start(x_in[t][:, :], x_tiles[t]).then_inc(x_landed[t], 16)
            with nc.allow_non_contiguous_dma(reason="per-feature vectors, once"):
                sp.dma_start(gain_in[:, :], subln_g[0].rearrange("(p o) -> p o", o=1)).then_inc(small_landed, 16)
                sp.dma_start(gate_bias[:, :], b_gate[0].rearrange("(t p) -> p t", p=PART)).then_inc(small_landed, 16)
                for c in range(C_TILES):
                    sp.dma_start(conv_taps[:, c, :], conv_w[0].rearrange("w (c p) -> c p w", p=PART)[c])\
                      .then_inc(small_landed, 16)
            for j in range(4):
                sp.wait_ge(tensor_done, T["x"].at(("x", j, 1), 0))
                sp.dma_start(x_in[j][:, :], x_tiles[4 + j]).then_inc(x_landed[j], 16)
            sp.wait_ge(const_made, 5)
            for n in (A_UNITS - 2, A_UNITS - 1):
                sp.dma_start(window_proj[n, :, 0:PART], zeros[:, :]).then_inc(zeros_stored, 16)
            with sp.Fori(0, B_HEADS) as h:
                for n, col in enumerate((COL_QB, COL_KB, COL_VB, COL_CC, COL_CU, COL_CB)):
                    load_item("heads", h, n, w_in_k[:, :, bass.ds(h * PART + col, PART)])
            with sp.Fori(0, A_UNITS // 2) as t:
                for e in range(2):
                    load_item("proj", t, e, w_in_k[:, :, bass.ds(t * (2 * PART) + e * PART, PART)])

            with sp.Fori(0, TILES // 2) as t:
                for e in range(2):
                    m = t * (2 * PART) + e * PART
                    load_item("window", t, 3 * e, w_gate_k[:, :, bass.ds(m + WIDTH, PART)])
                    load_item("window", t, 3 * e + 1, w_gate_k[:, :, bass.ds(m + 2 * WIDTH, PART)])
                    load_item("window", t, 3 * e + 2, w_branch_k[:, BRANCH_KT:3 * BRANCH_KT, bass.ds(m, PART)])
                    sp.wait_ge(vector_done, V["heads"].end)
                    sp.wait_ge(tensor_done, T["heads"].end)
                    for n in range(2):
                        sp.wait_ge(proj_stored[n], 16 * (1 + A_UNITS // 2))
                    sp.wait_ge(zeros_stored, 32)
                    sp.wait_ge(vector_done, V["window"].at(("qsplit", 1 - e, 1), t, back=1 - e))
                    sp.sem_inc(queries_seen, 1)
                    sp.wait_ge(tensor_done, T["window"].at(("vturn", 1 - e), t, back=1 - e))
                    sp.dma_start(qf[:, :, :], window_proj[0:4, :, bass.ds(m + PART, PART)]
                                 .rearrange("j p t -> p j t")).then_inc(window_landed, 16)
                    for r in range(2):
                        sp.dma_start(kf[HEAD * r:HEAD * r + HEAD, :, :],
                                     window_proj[4, :, bass.ds(m + CHUNK, WINDOW)]
                                     .rearrange("(v p) t -> p v t", p=HEAD)).then_inc(window_landed, 16)
                    sp.dma_start(vf[:, :], window_proj[5, :, bass.ds(m, 2 * PART)]).then_inc(window_landed, 16)

            with sp.Fori(0, KT // 2) as t:
                for e in range(2):
                    m = t * (2 * PART) + e * PART
                    load_item("merge", t, 3 * e, w_gate_k[:, :, bass.ds(m, PART)])
                    load_item("merge", t, 3 * e + 1, w_branch_k[:, 0:BRANCH_KT, bass.ds(m, PART)], BRANCH_KT)
                    load_item("merge", t, 3 * e + 2, w_out_k[:, :, bass.ds(m, PART)])
                    sp.wait_ge(merged_stored, 16 * (1 + KT))
                    sp.wait_ge(vector_done, V["window"].end)
                    sp.wait_ge(scalar_done, S["window"].end)
                    sp.wait_ge(tensor_done, T["window"].end)
                    sp.wait_ge(vector_done, V["merge"].at(("acc", e, 1), t, back=1))
                    sp.dma_start(merged[:, :, bass.ds(m, PART)],
                                 merged_bc[bass.ds(t * 2 + e, 1), :, :].rearrange("o p (t c) -> p (o t) c", c=PART))\
                      .then_inc(merged_landed[e], 16)

            load_item("ff", 0, 0, w_ffn_k[:, :, 0:PART])
            load_item("ff", 0, 1, w_ffn_k[:, :, D_FF:D_FF + PART])
            sp.wait_ge(vector_done, V["merge"].end)
            sp.wait_ge(units_done, BUFFERS + UNITS["ff"])
            sp.dma_start(ln_gain[:, :], ln1_g[0:1, :].partition_broadcast(PART)).then_inc(ln_landed, 16)
            sp.dma_start(ln_shift[:, :], ln1_b[0:1, :].partition_broadcast(PART)).then_inc(ln_landed, 16)
            sp.dma_start(x_res[:, :], x_tiles[0]).then_inc(res_landed, 16)
            with sp.Fori(0, 3) as t:
                for e in range(2):
                    sp.wait_ge(vector_done, V["res"].at(("r1", e), t))
                    sp.dma_start(x_res[:, :], x_tiles[bass.ds(t * 2 + (e + 1), 1)].rearrange("o p d -> (o p) d"))\
                      .then_inc(res_landed, 16)
            sp.wait_ge(vector_done, V["res7"].at(("r1", 0)))
            sp.dma_start(x_res[:, :], x_tiles[TILES - 1]).then_inc(res_landed, 16)

            def ff_items(t, skip):
                c = t * (2 * PART)
                cols = (c, c + D_FF, c + PART, c + (D_FF + PART))
                for n, col in enumerate(cols):
                    if n >= skip:
                        load_item("ff", t, n, w_ffn_k[:, :, bass.ds(col, PART)])
                for s in range(2):
                    load_item("ff", t, 4 + s, w_down_k[bass.ds(t * 2 + s, 1)]
                              .rearrange("o p (k c) -> (o p) k c", c=PART))

            ff_items(0, 2)
            sp.wait_ge(tensor_done, T["res7"].end)
            sp.dma_start(ln2_gain[:, :], ln2_g[0:1, :].partition_broadcast(PART)).then_inc(ln2_landed, 16)
            sp.dma_start(ln2_shift[:, :], ln2_b[0:1, :].partition_broadcast(PART)).then_inc(ln2_landed, 16)
            with sp.Fori(1, FF_TRIPS) as t:
                ff_items(t, 0)
            for t in range(TILES):
                sp.wait_ge(vector_done, V["end"].at(("b", t)))
                sp.dma_start(out_tiles[t], y_acc[:, t, :]).then_inc(out_stored, 16)
            sp.wait_ge(out_stored, 16 * TILES)

        @block.gpsimd
        def _(pool):
            pool.memset(ident[:, :], 0.0).then_inc(const_made, 1)
            pool.wait_ge(const_made, 1)
            pool.affine_select(out=ident[:, :], in_=ident[:, :], compare_op=ALU.not_equal, fill=1.0, base=0,
                               pattern=[[-1, PART]], channel_multiplier=1).then_inc(const_made, 1)
            pool.memset(rms_eps[:, :], EPS * RMS_SHIFT).then_inc(const_made, 1)
            pool.memset(ln_eps[:, :], EPS).then_inc(const_made, 1)
            pool.memset(zeros[:, :], 0.0).then_inc(const_made, 1)
            pool.iota(ramp_b[:, :], pattern=[[-1, TOKENS]], base=TOKENS - PART, channel_multiplier=1,
                      allow_small_or_imprecise_dtypes=True).then_inc(const_made, 1)
            pool.wait_ge(tensor_done, T["heads"].end)
            pool.wait_ge(vector_done, V["heads"].end)
            pool.wait_ge(scalar_done, S["heads"].end)
            pool.iota(ramp_a[:, :], pattern=[[-1, WINDOW]], base=CHUNK, channel_multiplier=1,
                      allow_small_or_imprecise_dtypes=True).then_inc(bias_a_made, 1)
            pool.wait_ge(bias_a_made, 1)
            pool.tensor_scalar(ramp_abs[:, :], ramp_a[:, :], -1.0, None, ALU.mult).then_inc(bias_a_made, 1)
            pool.wait_ge(bias_a_made, 2)
            pool.tensor_scalar(ramp_a[:, :], ramp_a[:, :], 0.0, None, ALU.max).then_inc(bias_a_made, 1)
            pool.wait_ge(bias_a_made, 3)
            pool.tensor_scalar(ramp_abs[:, :], ramp_abs[:, :], 0.0, None, ALU.max).then_inc(bias_a_made, 1)
            pool.wait_ge(bias_a_made, 4)
            pool.tensor_tensor(ramp_abs[:, :], ramp_abs[:, :], ramp_a[:, :], ALU.add).then_inc(bias_a_made, 1)
            pool.wait_ge(bias_a_made, 5)
            for h in range(A_HEADS):
                pool.tensor_scalar(bias_a[:, h, :], ramp_abs[:, :], 2.0 ** (-8.0 * (h + 1) / A_HEADS), None,
                                   ALU.mult).then_inc(bias_a_made, 1)
            pool.wait_ge(bias_a_made, 5 + A_HEADS)
            pool.tensor_copy(near_a[0:CHUNK, :, :], bias_a[0:CHUNK, :, 0:CHUNK]).then_inc(bias_a_made, 1)
            pool.wait_ge(bias_a_made, 6 + A_HEADS)
            pool.memset(bias_a[:, :, 0:CHUNK], MASKED).then_inc(bias_a_made, 1)
            pool.memset(bias_a[0:CHUNK, :, 2 * CHUNK:WINDOW], MASKED).then_inc(bias_a_made, 1)
            for g in range(2):
                pool.memset(a_prob[g][:, :, 0:CHUNK], 0.0).then_inc(bias_a_made, 1)

        @block.scalar
        def _(act):
            act.sem_inc(scalar_done, AHEAD)
            for n in range(2):
                act.sem_inc(proj_stored[n], 16)
            act.sem_inc(merged_stored, 16)

            def split_hi(stage, trip, n, dst, kts=KT, u=None):
                act.wait_ge(raw_landed[n % 2], landed(stage, trip, n))
                if u is not None:
                    act.wait_ge(units_done, u + 1)
                act.activation(dst, raw[n % 2][:, 0:kts, :], ACT.Copy).then_inc(weights_hi, 1)

            st = S["x"]
            with act.Fori(0, X_TRIPS) as t:
                for j in range(X_PER):
                    for hh in range(2):
                        act.wait_ge(tensor_done, T["x"].at(("x", j, hh), t))
                        act.activation(act_h[:, 4 * hh:4 * hh + 4, bass.ds(t * HALF + j * PART, PART)],
                                       bank[2 * (j % 2) + hh][:, :].rearrange("p (k c) -> p k c", c=PART),
                                       ACT.Copy).then_inc(scalar_done, st.step(("x", j, hh)))
            split_hi("heads", 0, 0, w_h[0][:, :, :], u=unit("heads", 0, 0))
            st = S["init"]
            act.wait_ge(vector_done, V["init"].at("l1"))
            act.activation(lam_exp[:, :], lam_sum[:, :], ACT.Exp).then_inc(scalar_done, st.step("le"))

            st = S["heads"]
            with act.Fori(0, B_HEADS) as h:
                for s in HEADS:
                    k, a = s[0], s[1:]
                    if k == "split":
                        n = a[0]
                        split_hi("heads", h, n, w_h[n % 2][:, :, :], u=unit("heads", h, n))
                    elif k == "out":
                        n, half = a
                        cols = slice(HALF * half, HALF * half + HALF)
                        b = bank[2 * (n % 2) + half]
                        if n in (0, 1, 2, 3):
                            if half == 0:
                                act.wait_ge(tensor_done, T["heads"].at(("half", n), h))
                            else:
                                act.wait_ge(units_done, unit("heads", h, n) + 1 + BUFFERS)
                        if n in (0, 1):
                            act.wait_ge(tensor_done, T["heads"].at(("scores", 7, 1), h, back=1))
                            act.activation((q_h, k_h)[n][:, cols], b[:, :], ACT.Copy,
                                           scale=(Q_SCALE, 1.0)[n]).then_inc(scalar_done, st.step(s))
                        elif n == 2:
                            act.activation(v_t[:, cols], b[:, :], ACT.Copy).then_inc(scalar_done, st.step(s))
                        elif n == 3:
                            act.wait_ge(vector_done, V["heads"].at(("out", 5, 1), h, back=1))
                            act.activation(conv[:, cols], b[:, :], ACT.Copy).then_inc(scalar_done, st.step(s))
                        elif n == 5:
                            act.wait_ge(vector_done, V["heads"].at(("gate", half), h))
                            act.activation(yc_h[:, bass.ds(h, 1), cols].rearrange("p o c -> p (o c)"), conv[:, cols],
                                           ACT.Copy).then_inc(scalar_done, st.step(s))
                    elif k == "scores" and a[1] == (a[0] >= 4):
                        i = a[0]
                        keys = PART * (i + 1)
                        last = ("peak", i) if i >= 4 else ("logit", i, 0, 1)
                        act.wait_ge(vector_done, V["heads"].at(last, h))
                        for m in range(2):
                            act.activation(prob[i % 2][m][:, 0:keys], prob[i % 2][m][:, 0:keys], ACT.Exp, scale=-1.0,
                                           bias=low[:, i % 2, m, 0:1], accum_out=den[:, i % 2, m:m + 1])\
                               .then_inc(scalar_done, st.step(("exp", i, m)))
                    elif k == "turn":
                        i, g = a
                        n = min(4, i + 1 - 4 * g)
                        act.wait_ge(tensor_done, T["heads"].at(s, h))
                        act.activation(wt_h[:, 4 * g:4 * g + n, :],
                                       bank[TURN][:, 0:PART * n].rearrange("p (k c) -> p k c", c=PART),
                                       ACT.Copy).then_inc(scalar_done, st.step(s))
                    elif k == "vturn":
                        g = a[0]
                        act.wait_ge(tensor_done, T["heads"].at(s, h))
                        act.activation(v_hl[:, 4 * g:4 * g + 4, 0:PART],
                                       bank[(TURN, VALUE)[g]][:, :].rearrange("p (k c) -> p k c", c=PART),
                                       ACT.Copy).then_inc(scalar_done, st.step(s))
                    elif k == "value":
                        i = a[0]
                        act.wait_ge(tensor_done, T["heads"].at(s, h))
                        if i:
                            act.wait_ge(vector_done, V["heads"].at(("sq", i - 1), h))
                        else:
                            act.wait_ge(vector_done, V["heads"].at(("sq", 7), h, back=1))
                        act.activation(o_tail[:, :], bank[VALUE][:, PART:2 * PART], ACT.Copy)\
                           .then_inc(scalar_done, st.step(("tail", i)))
                    elif k == "rms":
                        act.wait_ge(vector_done, V["heads"].at(("sq", 7), h))
                        act.activation(rms_root[:, :], square_sum[:, :], ACT.Sqrt, scale=RMS_SHIFT / PART,
                                       bias=rms_eps[:, 0:1]).then_inc(scalar_done, st.step(("root",)))
                    elif k == "yturn":
                        g = a[0]
                        act.wait_ge(tensor_done, T["heads"].at(s, h))
                        act.activation(yb_h[:, bass.ds(h, 1), HALF * g:HALF * g + HALF].rearrange("p o c -> p (o c)"),
                                       bank[(TURN, VALUE)[g]][:, :], ACT.Copy, scale=rms_gain[:, 0:1])\
                           .then_inc(scalar_done, st.step(s))

            st = S["proj"]
            act.wait_ge(vector_done, V["heads"].end)
            with act.Fori(0, A_UNITS // 2) as t:
                for e in range(2):
                    split_hi("proj", t, e + 1, w_h[(e + 1) % 2][:, :, :], u=unit("proj", t, e + 1))
                    act.wait_ge(proj_stored[e], t * 16 + 16)
                    for half in range(2):
                        if half == 0:
                            act.wait_ge(tensor_done, T["proj"].at(("half", e), t))
                        else:
                            act.wait_ge(units_done, unit("proj", t, e) + 1 + BUFFERS)
                        act.activation(to_dram[e][:, HALF * half:HALF * half + HALF], bank[2 * e + half][:, :],
                                       ACT.Copy).then_inc(scalar_done, st.step(("out", e, half)))
                    act.wait_ge(scalar_done, st.at(("out", e, 1), t))
                    act.dma_start(window_proj[bass.ds(t * 2 + e, 1), :, PART:PART + TOKENS]
                                  .rearrange("o p t -> (o p) t"), to_dram[e][:, :]).then_inc(proj_stored[e], 16)

            st = S["window"]
            act.wait_ge(bias_a_made, 10 + A_HEADS)
            with act.Fori(0, TILES // 2) as t:
                for s in WIN:
                    k, e, a = s[0], s[1], s[2:]
                    if k == "split":
                        n = e
                        split_hi("window", t, n, w_h[n % 2][:, :, :], u=unit("window", t, n))
                    elif k == "out" and a[0] < 2:
                        n, half = a
                        b = bank[2 * n + half]
                        if half == 0:
                            act.wait_ge(tensor_done, T["window"].at(("part", e, n, 24), t))
                        else:
                            act.wait_ge(units_done, unit("window", t, 3 * e + n) + 1 + BUFFERS)
                        if n == 0 and half == 0:
                            act.wait_ge(merged_stored, t * 32 + 16 * (e + 1))
                        act.sem_inc(gates_seen, 1)
                        act.activation((sig_b, sig_c)[n][:, HALF * half:HALF * half + HALF], b[:, :], ACT.Sigmoid,
                                       bias=gate_bias[:, bass.ds(t * 2 + (e + KT * (n + 1)), 1)])\
                           .then_inc(scalar_done, st.step(s))
                    elif k == "ksplit":
                        act.wait_ge(window_landed, t * 128 + 64 * (e + 1))
                        act.wait_ge(tensor_done, T["window"].at(("scores", 1 - e, 1), t, back=1 - e))
                        act.activation(ks_h[:, :, :], kf[:, :, :], ACT.Copy).then_inc(scalar_done, st.step(s))
                    elif k == "qsplit":
                        g = a[0]
                        if g:
                            act.wait_ge(tensor_done, T["window"].at(("scores", e, 0), t))
                        act.activation(qs_h[:, :, :], qf[:, 2 * g:2 * g + 2, :], ACT.Copy, scale=Q_SCALE)\
                           .then_inc(scalar_done, st.step(s))
                    elif k == "vturn":
                        act.wait_ge(tensor_done, T["window"].at(s, t))
                        act.activation(vs_hl[:, :, :, 0:HEAD],
                                       bank[TURN][:, 0:2 * PART].rearrange("p (b v c) -> p b v c", b=2, v=2),
                                       ACT.Copy).then_inc(scalar_done, st.step(s))
                    elif k == "scores":
                        g = a[0]
                        for n in range(A_GROUP):
                            act.wait_ge(vector_done, V["window"].at(("logit", e, g, n), t))
                            act.activation(a_prob[g][:, n, CHUNK:2 * PART], a_prob[g][:, n, CHUNK:2 * PART], ACT.Exp,
                                           scale=-1.0, bias=a_low[:, 4 * g + n:4 * g + n + 1],
                                           accum_out=a_den[:, 4 * g + n:4 * g + n + 1])\
                               .then_inc(scalar_done, st.step(("exp", e, g, n)))
                        act.wait_ge(vector_done, V["window"].at(("sub", e, g), t))
                        act.activation(a_sunk[:, 4 * g:4 * g + 4], a_sink[:, 4 * g:4 * g + 4], ACT.Exp)\
                           .then_inc(scalar_done, st.step(("sink", e, g)))
                    elif k == "turn":
                        act.wait_ge(tensor_done, T["window"].at(s, t))
                        act.activation(at_h[:, :, :], bank[TURN][:, :].rearrange("p (k c) -> p k c", c=PART),
                                       ACT.Copy).then_inc(scalar_done, st.step(s))
                    elif k == "norm":
                        g = a[0]
                        act.wait_ge(tensor_done, T["window"].at(("value", e, g, 1), t))
                        act.activation(a_tail[:, :, :], bank[VALUE][:, :].rearrange("p (n c) -> p n c", c=2 * HEAD)
                                       [:, :, HEAD:2 * HEAD], ACT.Copy).then_inc(scalar_done, st.step(("tail", e, g)))
                    elif k == "yturn":
                        g = a[0]
                        act.wait_ge(tensor_done, T["window"].at(s, t))
                        act.activation(ya_h[:, 2 * g:2 * g + 2, bass.ds(t * (2 * PART) + e * PART, PART)],
                                       bank[TURN][:, 0:2 * PART].rearrange("p (k c) -> p k c", c=PART),
                                       ACT.Copy).then_inc(scalar_done, st.step(s))
                    elif k == "store":
                        act.wait_ge(vector_done, V["window"].at(("add", e), t))
                        act.dma_start(merged_bc[bass.ds(t * 2 + e, 1), :, :].rearrange("o p t -> (o p) t"),
                                      sig_b[:, :]).then_inc(merged_stored, 16)

            st = S["merge"]
            with act.Fori(0, KT // 2) as t:
                for e in range(2):
                    for n in range(2):
                        m = 3 * e + n + 1
                        if n == 0:
                            split_hi("merge", t, m, w_h[1][:, 0:BRANCH_KT, :], BRANCH_KT,
                                     u=unit("merge", t, 2 * e + 1))
                            for half in range(2):
                                if half == 0:
                                    act.wait_ge(tensor_done, T["merge"].at(("part", e, 0), t))
                                    act.wait_ge(vector_done, V["merge"].at(("acc", 1 - e, 1), t, back=1 - e))
                                else:
                                    act.wait_ge(units_done, unit("merge", t, 2 * e) + 1 + BUFFERS)
                                act.sem_inc(gates_seen, 1)
                                act.activation(sig_a[:, HALF * half:HALF * half + HALF], bank[half][:, :], ACT.Sigmoid,
                                               bias=gate_bias[:, bass.ds(t * 2 + e, 1)])\
                                   .then_inc(scalar_done, st.step(("out", e, half)))
                        else:
                            split_hi("merge", t, m, wo_h[:, :, bass.ds(t * (2 * PART) + e * PART, PART)])
                            split_hi("merge", t, m + 1, w_h[0][:, :, :], u=unit("merge", t, 2 * e + 2))

            def merged_hi(stage, label, e, tile):
                act.activation(m_h[e][:, :, :], merged[:, tile, :].rearrange("p (k c) -> p k c", c=PART), ACT.Copy)\
                   .then_inc(scalar_done, S[stage].step(label))

            act.wait_ge(vector_done, V["merge"].end)
            act.wait_ge(units_done, BUFFERS + UNITS["ff"])
            merged_hi("res0", "ms0", 0, 0)
            merged_hi("res0", "ms1", 1, 1)

            def norm_scalar(stage, lab, trip, tile, slot):
                act.wait_ge(vector_done, V[stage].at(("ag", lab), trip))
                act.activation(ln_root[:, :], moments[:, 1:2], ACT.Sqrt, bias=ln_eps[:, 0:1])\
                   .then_inc(scalar_done, S[stage].step(("root", lab)))
                act.wait_ge(vector_done, V[stage].at(("b", lab), trip))
                act.activation(y_acc[:, bass.ds(tile, 1), :].rearrange("p o c -> p (o c)"), normed[slot][:, :], ACT.Copy,
                               scale=ALPHA).then_inc(scalar_done, S[stage].step(("keep", lab)))

            def norm_turned(stage, lab, trip, tile):
                for g in range(2):
                    act.wait_ge(tensor_done, T[stage].at((f"turn{g}", lab), trip))
                    act.activation(act_h[:, 4 * g:4 * g + 4, bass.ds(tile * PART, PART)],
                                   bank[(TURN, VALUE)[g]][:, :].rearrange("p (k c) -> p k c", c=PART),
                                   ACT.Copy).then_inc(scalar_done, S[stage].step((f"turn{g}", lab)))

            with act.Fori(0, 3) as t:
                for e in range(2):
                    if e == 0:
                        act.wait_ge(tensor_done, T["res"].at(("m1", 1), t, back=1))
                        act.wait_ge(tensor_done, T["res0"].end)
                    else:
                        act.wait_ge(tensor_done, T["res"].at(("m1", 0), t))
                    act.activation(m_h[e][:, :, :].rearrange("p k c -> p (k c)"),
                                   merged[:, bass.ds(t * 2 + (e + 2), 1), :].rearrange("p o c -> p (o c)"),
                                   ACT.Copy).then_inc(scalar_done, S["res"].step(("ms", e)))
                    norm_scalar("res", e, t, t * 2 + e, e)
                    norm_turned("res", e, t, t * 2 + e)
            norm_scalar("res7", 0, 0, 6, 0)
            norm_turned("res7", 0, 0, 6)
            norm_scalar("res7", "t", 0, 7, 1)
            norm_turned("res7", "t", 0, 7)

            def ff(t, last):
                st = S["ff"]
                for s in range(2):
                    split_hi("ff", t, 2 * s + 1, w_h[1][:, :, :], u=unit("ff", t, 2 * s + 1))
                    for half in range(2):
                        act.wait_ge(tensor_done, T["ff"].at(("half", 2 * s), t)) if half == 0 else \
                            act.wait_ge(units_done, unit("ff", t, 2 * s) + 1 + BUFFERS)
                        act.wait_ge(vector_done, V["ff"].at(("lo", 1 - s, half), t, back=1 - s))
                        act.activation(silu[:, HALF * half:HALF * half + HALF], bank[half][:, :], ACT.Silu)\
                           .then_inc(scalar_done, st.step(("silu", s, half)))
                    if s == 0:
                        split_hi("ff", t, 2, w_h[0][:, :, :], u=unit("ff", t, 2))
                    else:
                        for d in range(2):
                            if d == 0:
                                act.wait_ge(tensor_done, T["ff"].at(("down", TILES - 1, 1), t, back=1))
                            split_hi("ff", t, 4 + d, wd_h[d][:, :].rearrange("p (k c) -> p k c", c=PART))
                    for half in range(2):
                        act.wait_ge(vector_done, V["ff"].at(("up", s, half), t))
                        act.activation(h_h[s][:, HALF * half:HALF * half + HALF],
                                       silu[:, HALF * half:HALF * half + HALF], ACT.Copy)\
                           .then_inc(scalar_done, st.step(("hi", s, half)))
                if not last:
                    split_hi("ff", t, 6, w_h[0][:, :, :], u=unit("ff", t, 4))

            act.wait_ge(tensor_done, T["res7"].end)
            with act.Fori(0, FF_TRIPS - 1) as t:
                ff(t, False)
            ff(FF_TRIPS - 1, True)
            for t in range(TILES):
                act.wait_ge(vector_done, V["end"].at(("ag", t)))
                act.activation(ln_root[:, :], moments[:, 1:2], ACT.Sqrt, bias=ln_eps[:, 0:1])\
                   .then_inc(scalar_done, S["end"].step(("root", t)))

        @block.vector
        def _(dve):
            dve.sem_inc(vector_done, AHEAD)
            dve.sem_inc(weights_ready, BUFFERS)

            def f32(ap):
                return ap.bitcast(F32)

            def split_lo(stage, trip, n, hi, lo, kts=KT):
                dve.wait_ge(weights_hi, item(stage, trip, n) + 1)
                dve.tensor_tensor(lo, raw[n % 2][:, 0:kts, :], f32(hi), ALU.subtract).then_inc(weights_ready, 1)

            st = V["x"]
            with dve.Fori(0, X_TRIPS) as t:
                for j in range(X_PER):
                    for hh in range(2):
                        cols = bass.ds(t * HALF + j * PART, PART)
                        dve.wait_ge(scalar_done, S["x"].at(("x", j, hh), t))
                        dve.tensor_tensor(act_l[:, 4 * hh:4 * hh + 4, cols],
                                          bank[2 * (j % 2) + hh][:, :].rearrange("p (k c) -> p k c", c=PART),
                                          f32(act_h[:, 4 * hh:4 * hh + 4, cols]), ALU.subtract)\
                           .then_inc(vector_done, st.step(("x", j, hh)))
            split_lo("heads", 0, 0, w_h[0][:, :, :], w_l[0][:, :, :])
            st = V["init"]
            dve.wait_ge(small_landed, 16 * (7 + C_TILES))
            for n in range(2):
                dve.tensor_tensor_reduce(out=lam_out[:, n, :], in0=lam_in[:, 2 * n, :], in1=lam_in[:, 2 * n + 1, :],
                                         scale=1.0, scalar=0.0, op0=ALU.mult, op1=ALU.add,
                                         accum_out=lam_sum[:, n:n + 1]).then_inc(vector_done, st.step(f"l{n}"))
            dve.wait_ge(scalar_done, S["init"].at("le"))
            dve.tensor_tensor(neg_lam[:, :], lam_exp[:, 0:1], lam_exp[:, 1:2], ALU.subtract)\
               .then_inc(vector_done, st.step("dl"))
            dve.wait_ge(vector_done, st.at("dl"))
            dve.tensor_scalar(neg_lam[:, :], neg_lam[:, :], LAMBDA_INIT, -1.0, ALU.add, ALU.mult)\
               .then_inc(vector_done, st.step("nl"))
            dve.tensor_scalar(rms_gain[:, :], gain_in[:, :], 1.0 - LAMBDA_INIT, None, ALU.mult)\
               .then_inc(vector_done, st.step("gain"))
            dve.tensor_scalar(neg_sink[:, :], sink_in[:, :], -1.0, None, ALU.mult)\
               .then_inc(vector_done, st.step("sink"))
            dve.wait_ge(const_made, 6)
            dve.scalar_tensor_tensor(out=bias_b[:, :], in0=ramp_b[:, :], scalar=-1.0, in1=ramp_b[:, :], op0=ALU.mult,
                                     op1=ALU.max).then_inc(vector_done, st.step("ramp"))
            dve.wait_ge(vector_done, st.at("ramp"))
            dve.memset(bias_b[0:CHUNK, TOKENS - CHUNK:TOKENS], MASKED).then_inc(const_made, 1)
            dve.memset(gated[:, 0:2], 0.0).then_inc(const_made, 1)

            st = V["heads"]
            dve.wait_ge(const_made, 8)
            dve.wait_ge(zeros_stored, 32)
            with dve.Fori(0, B_HEADS) as h:
                for s in HEADS:
                    k, a = s[0], s[1:]
                    if k == "split":
                        n = a[0]
                        split_lo("heads", h, n, w_h[n % 2][:, :, :], w_l[n % 2][:, :, :])
                    elif k == "decay":
                        dve.wait_ge(vector_done, st.at(("logit", 7, 1, 1), h, back=1))
                        dve.tensor_scalar(bias_b[:, :], bias_b[:, :], 2.0 ** (-8.0 / B_HEADS), None, ALU.mult)\
                           .then_inc(vector_done, st.step(s))
                    elif k == "out":
                        n, half = a
                        cols = slice(HALF * half, HALF * half + HALF)
                        b = bank[2 * (n % 2) + half]
                        if n in (0, 1):
                            dve.wait_ge(scalar_done, S["heads"].at(s, h))
                            if n == 0:
                                dve.scalar_tensor_tensor(out=q_l[:, cols], in0=b[:, :], scalar=Q_SCALE,
                                                         in1=f32(q_h[:, cols]), op0=ALU.mult, op1=ALU.subtract)\
                                   .then_inc(vector_done, st.step(s))
                            else:
                                dve.tensor_tensor(k_l[:, cols], b[:, :], f32(k_h[:, cols]), ALU.subtract)\
                                   .then_inc(vector_done, st.step(s))
                        elif n == 4:
                            dve.wait_ge(scalar_done, S["heads"].at(("out", 3, half), h))
                            if half == 0:
                                dve.wait_ge(tensor_done, T["heads"].at(("half", 4), h))
                                dve.wait_ge(vector_done, st.at(("conv", 2), h, back=1))
                            else:
                                dve.wait_ge(units_done, unit("heads", h, 4) + 1 + BUFFERS)
                            dve.tensor_tensor(gated[:, 2 + HALF * half:2 + HALF * half + HALF], b[:, :], conv[:, cols],
                                              ALU.mult).then_inc(vector_done, st.step(s))
                        elif n == 5:
                            if half == 0:
                                dve.wait_ge(tensor_done, T["heads"].at(("half", 5), h))
                                dve.wait_ge(vector_done, st.at(("conv", 2), h))
                            else:
                                dve.wait_ge(units_done, unit("heads", h, 5) + 1 + BUFFERS)
                            dve.tensor_tensor(conv[:, cols], b[:, :], conv[:, cols], ALU.mult)\
                               .then_inc(vector_done, st.step(("gate", half)))
                            dve.wait_ge(scalar_done, S["heads"].at(s, h))
                            tile = bass.ds(h, 1)
                            dve.tensor_tensor(yc_l[:, tile, cols].rearrange("p o c -> p (o c)"), conv[:, cols],
                                              f32(yc_h[:, tile, cols].rearrange("p o c -> p (o c)")), ALU.subtract)\
                               .then_inc(vector_done, st.step(s))
                    elif k == "conv":
                        tap = [conv_taps[:, bass.ds(h, 1), w:w + 1].rearrange("p o w -> p (o w)") for w in range(3)]
                        dve.wait_ge(vector_done, st.at(("out", 4, 1), h))
                        dve.tensor_scalar(conv[:, :], gated[:, 0:TOKENS], tap[0], None, ALU.mult)\
                           .then_inc(vector_done, st.step(("conv", 0)))
                        for w in (1, 2):
                            dve.wait_ge(vector_done, st.at(("conv", w - 1), h))
                            dve.scalar_tensor_tensor(out=conv[:, :], in0=gated[:, w:w + TOKENS], scalar=tap[w],
                                                     in1=conv[:, :], op0=ALU.mult, op1=ALU.add)\
                               .then_inc(vector_done, st.step(("conv", w)))
                    elif k == "scores":
                        i, c = a
                        keys = min(HALF, PART * (i + 1) - HALF * c)
                        off = PART * (7 - i) + HALF * c
                        dve.wait_ge(tensor_done, T["heads"].at(s, h))
                        dve.sem_inc(scores_seen, 1)
                        for m in range(2):
                            dve.tensor_tensor_reduce(out=prob[i % 2][m][:, HALF * c:HALF * c + keys],
                                                     in0=bank[SCORES[m]][:, 0:keys], in1=bias_b[:, off:off + keys],
                                                     scale=1.0, scalar=3e38, op0=ALU.add, op1=ALU.min,
                                                     accum_out=low[:, i % 2, m, c:c + 1])\
                               .then_inc(vector_done, st.step(("logit", i, c, m)))
                        if c == 1:
                            dve.wait_ge(vector_done, st.at(("logit", i, 1, 1), h))
                            dve.tensor_tensor(low[:, i % 2, :, 0], low[:, i % 2, :, 0], low[:, i % 2, :, 1], ALU.min)\
                               .then_inc(vector_done, st.step(("peak", i)))
                    elif k == "mix":
                        i = a[0]
                        p, keys = i % 2, PART * (i + 1)
                        dve.wait_ge(scalar_done, S["heads"].at(("exp", i, 1), h))
                        dve.reciprocal(inv[:, p, :], den[:, p, :]).then_inc(vector_done, st.step(("inv", i)))
                        dve.wait_ge(vector_done, st.at(("inv", i), h))
                        dve.tensor_scalar(prob[p][0][:, 0:keys], prob[p][0][:, 0:keys], inv[:, p, 0:1], None, ALU.mult)\
                           .then_inc(vector_done, st.step(("norm", i)))
                        dve.tensor_tensor(inv[:, p, 1:2], inv[:, p, 1:2], neg_lam[:, :], ALU.mult)\
                           .then_inc(vector_done, st.step(("lam", i)))
                        dve.wait_ge(vector_done, st.at(("lam", i), h))
                        dve.scalar_tensor_tensor(out=prob[p][0][:, 0:keys], in0=prob[p][1][:, 0:keys],
                                                 scalar=inv[:, p, 1:2], in1=prob[p][0][:, 0:keys], op0=ALU.mult,
                                                 op1=ALU.add).then_inc(vector_done, st.step(("mix", i)))
                    elif k == "turn":
                        i, g = a
                        n = min(4, i + 1 - 4 * g)
                        dve.wait_ge(scalar_done, S["heads"].at(s, h))
                        dve.tensor_tensor(wt_l[:, 4 * g:4 * g + n, :],
                                          bank[TURN][:, 0:PART * n].rearrange("p (k c) -> p k c", c=PART),
                                          f32(wt_h[:, 4 * g:4 * g + n, :]), ALU.subtract)\
                           .then_inc(vector_done, st.step(s))
                    elif k == "vturn":
                        g = a[0]
                        dve.wait_ge(scalar_done, S["heads"].at(s, h))
                        dve.tensor_tensor(v_hl[:, 4 * g:4 * g + 4, PART:2 * PART],
                                          bank[(TURN, VALUE)[g]][:, :].rearrange("p (k c) -> p k c", c=PART),
                                          f32(v_hl[:, 4 * g:4 * g + 4, 0:PART]), ALU.subtract)\
                           .then_inc(vector_done, st.step(s))
                    elif k == "value":
                        i = a[0]
                        dve.wait_ge(scalar_done, S["heads"].at(("tail", i), h))
                        dve.tensor_tensor(mixed[:, i, :], bank[VALUE][:, 0:PART], o_tail[:, :], ALU.add)\
                           .then_inc(vector_done, st.step(("sum", i)))
                        dve.wait_ge(vector_done, st.at(("sum", i), h))
                        dve.tensor_tensor_reduce(out=o_tail[:, :], in0=mixed[:, i, :], in1=mixed[:, i, :], scale=1.0,
                                                 scalar=0.0, op0=ALU.mult, op1=ALU.add,
                                                 accum_out=square_sum[:, i:i + 1])\
                           .then_inc(vector_done, st.step(("sq", i)))
                    elif k == "rms":
                        dve.wait_ge(scalar_done, S["heads"].at(("root",), h))
                        dve.reciprocal(rms_inv[:, :], rms_root[:, :]).then_inc(vector_done, st.step(("rinv",)))
                        dve.wait_ge(vector_done, st.at(("rinv",), h))
                        dve.tensor_scalar(rms_inv[:, :], rms_inv[:, :], RMS_SHIFT ** 0.5, None, ALU.mult)\
                           .then_inc(vector_done, st.step(("rscale",)))
                        dve.wait_ge(vector_done, st.at(("rscale",), h))
                        dve.tensor_tensor(mixed[:, :, :], mixed[:, :, :],
                                          rms_inv[:, :].rearrange("p (t o) -> p t o", o=1)
                                          .to_broadcast([PART, TILES, PART]), ALU.mult)\
                           .then_inc(vector_done, st.step(("rmul",)))
                    elif k == "yturn":
                        g = a[0]
                        tile = bass.ds(h, 1)
                        dve.wait_ge(scalar_done, S["heads"].at(s, h))
                        cols = slice(HALF * g, HALF * g + HALF)
                        dve.scalar_tensor_tensor(out=yb_l[:, tile, cols].rearrange("p o c -> p (o c)"),
                                                 in0=bank[(TURN, VALUE)[g]][:, :], scalar=rms_gain[:, 0:1],
                                                 in1=f32(yb_h[:, tile, cols].rearrange("p o c -> p (o c)")),
                                                 op0=ALU.mult, op1=ALU.subtract).then_inc(vector_done, st.step(s))

            with dve.Fori(0, A_UNITS // 2) as t:
                for e in range(2):
                    split_lo("proj", t, e + 1, w_h[(e + 1) % 2][:, :, :], w_l[(e + 1) % 2][:, :, :])

            st = V["window"]
            dve.wait_ge(bias_a_made, 10 + A_HEADS)
            with dve.Fori(0, TILES // 2) as t:
                for s in WIN:
                    k, e, a = s[0], s[1], s[2:]
                    if k == "split":
                        n = e
                        split_lo("window", t, n, w_h[n % 2][:, :, :], w_l[n % 2][:, :, :])
                    elif k == "out" and a[0] == 2:
                        q = a[1]
                        br, half = divmod(q, 2)
                        if q < 3:
                            dve.wait_ge(tensor_done, T["window"].at(("part", e, 2, 12 * (q + 1)), t))
                        else:
                            dve.wait_ge(units_done, unit("window", t, 3 * e + 2) + 1 + BUFFERS)
                        cols = slice(HALF * half, HALF * half + HALF)
                        sig = (sig_b, sig_c)[br]
                        dve.wait_ge(scalar_done, S["window"].at(("out", e, br, half), t))
                        dve.tensor_tensor(sig[:, cols], bank[2 * br + half][:, :], sig[:, cols], ALU.mult)\
                           .then_inc(vector_done, st.step(s))
                    elif k == "ksplit":
                        dve.wait_ge(scalar_done, S["window"].at(s, t))
                        dve.tensor_tensor(ks_l[:, :, :], kf[:, :, :], f32(ks_h[:, :, :]), ALU.subtract)\
                           .then_inc(vector_done, st.step(s))
                    elif k == "qsplit":
                        g = a[0]
                        dve.wait_ge(scalar_done, S["window"].at(s, t))
                        dve.scalar_tensor_tensor(out=qs_l[:, :, :], in0=qf[:, 2 * g:2 * g + 2, :], scalar=Q_SCALE,
                                                 in1=f32(qs_h[:, :, :]), op0=ALU.mult, op1=ALU.subtract)\
                           .then_inc(vector_done, st.step(s))
                    elif k == "vturn":
                        dve.wait_ge(scalar_done, S["window"].at(s, t))
                        dve.tensor_tensor(vs_hl[:, :, :, HEAD:2 * HEAD],
                                          bank[TURN][:, 0:2 * PART].rearrange("p (b v c) -> p b v c", b=2, v=2),
                                          f32(vs_hl[:, :, :, 0:HEAD]), ALU.subtract).then_inc(vector_done, st.step(s))
                    elif k == "scores":
                        g = a[0]
                        dve.wait_ge(tensor_done, T["window"].at(s, t))
                        dve.sem_inc(scores_seen, 1)
                        for n in range(A_GROUP):
                            hd = A_GROUP * g + n
                            dve.tensor_tensor_reduce(out=a_prob[g][:, n, CHUNK:2 * PART],
                                                     in0=bank[SCORES[n % 2]][:, WINDOW * (n // 2):WINDOW * (n // 2) + WINDOW],
                                                     in1=bias_a[:, hd, :], scale=1.0, scalar=neg_sink[:, hd:hd + 1],
                                                     op0=ALU.add, op1=ALU.min, accum_out=a_low[:, hd:hd + 1])\
                               .then_inc(vector_done, st.step(("logit", e, g, n)))
                        dve.wait_ge(vector_done, st.at(("logit", e, g, 3), t))
                        dve.tensor_tensor(a_sink[:, 4 * g:4 * g + 4], a_low[:, 4 * g:4 * g + 4],
                                          neg_sink[:, 4 * g:4 * g + 4], ALU.subtract)\
                           .then_inc(vector_done, st.step(("sub", e, g)))
                    elif k == "turn":
                        dve.wait_ge(scalar_done, S["window"].at(s, t))
                        dve.tensor_tensor(at_l[:, :, :], bank[TURN][:, :].rearrange("p (k c) -> p k c", c=PART),
                                          f32(at_h[:, :, :]), ALU.subtract).then_inc(vector_done, st.step(s))
                    elif k == "norm":
                        g = a[0]
                        hd = slice(4 * g, 4 * g + 4)
                        dve.wait_ge(scalar_done, S["window"].at(("tail", e, g), t))
                        dve.tensor_tensor(a_inv[:, hd], a_den[:, hd], a_sunk[:, hd], ALU.add)\
                           .then_inc(vector_done, st.step(("den", e, g)))
                        dve.wait_ge(vector_done, st.at(("den", e, g), t))
                        dve.reciprocal(a_inv[:, hd], a_inv[:, hd]).then_inc(vector_done, st.step(("inv", e, g)))
                        dve.wait_ge(vector_done, st.at(("yturn", e, 0), t) if g else
                                    st.at(("yturn", 1 - e, 1), t, back=1 - e))
                        dve.tensor_tensor(a_mix[:, :, :], bank[VALUE][:, :].rearrange("p (n c) -> p n c", c=2 * HEAD)
                                          [:, :, 0:HEAD], a_tail[:, :, :], ALU.add)\
                           .then_inc(vector_done, st.step(("sum", e, g)))
                        dve.wait_ge(vector_done, st.at(("sum", e, g), t))
                        dve.tensor_tensor(a_mix[:, :, :], a_mix[:, :, :],
                                          a_inv[:, hd].rearrange("p (t o) -> p t o", o=1)
                                          .to_broadcast([PART, A_GROUP, HEAD]), ALU.mult)\
                           .then_inc(vector_done, st.step(("norm", e, g)))
                    elif k == "yturn":
                        g = a[0]
                        cols = bass.ds(t * (2 * PART) + e * PART, PART)
                        dve.wait_ge(scalar_done, S["window"].at(s, t))
                        dve.tensor_tensor(ya_l[:, 2 * g:2 * g + 2, cols],
                                          bank[TURN][:, 0:2 * PART].rearrange("p (k c) -> p k c", c=PART),
                                          f32(ya_h[:, 2 * g:2 * g + 2, cols]), ALU.subtract)\
                           .then_inc(vector_done, st.step(s))
                    elif k == "unmask":
                        dve.wait_ge(vector_done, st.at(("logit", e, 1, 3), t))
                        dve.tensor_copy(bias_a[0:CHUNK, :, 0:CHUNK], near_a[0:CHUNK, :, :])\
                           .then_inc(vector_done, st.step(s))
                    elif k == "add":
                        dve.wait_ge(vector_done, st.at(("out", e, 2, 3), t))
                        dve.tensor_tensor(sig_b[:, :], sig_b[:, :], sig_c[:, :], ALU.add)\
                           .then_inc(vector_done, st.step(s))

            st = V["merge"]
            with dve.Fori(0, KT // 2) as t:
                for e in range(2):
                    split_lo("merge", t, 3 * e + 1, w_h[1][:, 0:BRANCH_KT, :], w_l[1][:, 0:BRANCH_KT, :], BRANCH_KT)
                    m = bass.ds(t * (2 * PART) + e * PART, PART)
                    split_lo("merge", t, 3 * e + 2, wo_h[:, :, m], wo_l[:, :, m])
                    split_lo("merge", t, 3 * e + 3, w_h[0][:, :, :], w_l[0][:, :, :])
                    for half in range(2):
                        if half == 0:
                            dve.wait_ge(tensor_done, T["merge"].at(("part", e, 1), t))
                            dve.wait_ge(merged_landed[e], t * 16 + 16)
                        else:
                            dve.wait_ge(units_done, unit("merge", t, 2 * e + 1) + 1 + BUFFERS)
                        cols = slice(HALF * half, HALF * half + HALF)
                        dve.wait_ge(scalar_done, S["merge"].at(("out", e, half), t))
                        dve.tensor_tensor(sig_a[:, cols], bank[2 + half][:, :], sig_a[:, cols], ALU.mult)\
                           .then_inc(vector_done, st.step(("mul", e, half)))
                        dve.wait_ge(vector_done, st.at(("mul", e, half), t))
                        part = merged[:, 4 * half:4 * half + 4, m]
                        dve.tensor_tensor(part, part, sig_a[:, cols].rearrange("p (t c) -> p t c", c=PART), ALU.add)\
                           .then_inc(vector_done, st.step(("acc", e, half)))

            def merged_lo(stage, label, e, tile, trip=0):
                dve.wait_ge(scalar_done, S[stage].at(label, trip))
                dve.tensor_tensor(m_l[e][:, :, :].rearrange("p k c -> p (k c)"), tile,
                                  f32(m_h[e][:, :, :].rearrange("p k c -> p (k c)")), ALU.subtract)\
                   .then_inc(vector_done, V[stage].step(label))

            merged_lo("res0", "ms0", 0, merged[:, 0, :])
            merged_lo("res0", "ms1", 1, merged[:, 1, :])
            dve.wait_ge(ln_landed, 32)

            def layer_norm(stage, lab, trip, y, gain, shift):
                st = V[stage]
                for half in range(2):
                    dve.bn_stats(stats[:, half, :], y[:, HALF * half:HALF * half + HALF])\
                       .then_inc(vector_done, st.step((f"st{half}", lab)))
                dve.wait_ge(vector_done, st.at(("st1", lab), trip))
                dve.sem_inc(moments_seen, 1)
                dve.bn_aggr(moments[:, :], stats[:, :, :].rearrange("p a b -> p (a b)"))\
                   .then_inc(vector_done, st.step(("ag", lab)))
                dve.wait_ge(scalar_done, S[stage].at(("root", lab), trip))
                dve.reciprocal(ln_inv[:, :], ln_root[:, :]).then_inc(vector_done, st.step(("ri", lab)))
                dve.wait_ge(vector_done, st.at(("ri", lab), trip))
                dve.tensor_scalar(y, y, moments[:, 0:1], ln_inv[:, 0:1], ALU.subtract, ALU.mult)\
                   .then_inc(vector_done, st.step(("z", lab)))
                dve.wait_ge(vector_done, st.at(("z", lab), trip))
                dve.tensor_tensor(y, y, gain[:, :], ALU.mult).then_inc(vector_done, st.step(("g", lab)))
                dve.wait_ge(vector_done, st.at(("g", lab), trip))
                dve.tensor_tensor(y, y, shift[:, :], ALU.add).then_inc(vector_done, st.step(("b", lab)))

            def residual(stage, lab, trip, slot, landed_at, done0, done1):
                for half, done in enumerate((done0, done1)):
                    cols = slice(HALF * half, HALF * half + HALF)
                    if half == 0:
                        dve.wait_ge(res_landed, landed_at)
                    for d in done:
                        dve.wait_ge(tensor_done, d)
                    dve.scalar_tensor_tensor(out=normed[slot][:, cols], in0=x_res[:, cols], scalar=ALPHA,
                                             in1=bank[2 * slot + half][:, :], op0=ALU.mult, op1=ALU.add)\
                       .then_inc(vector_done, V[stage].step((f"r{half}", lab)))
                dve.wait_ge(vector_done, V[stage].at(("r1", lab), trip))

            def norm(stage, lab, trip, slot):
                layer_norm(stage, lab, trip, normed[slot][:, :], ln_gain, ln_shift)

            def turned_lo(stage, lab, trip, tile):
                for g in range(2):
                    cols = bass.ds(tile * PART, PART)
                    dve.wait_ge(scalar_done, S[stage].at((f"turn{g}", lab), trip))
                    dve.tensor_tensor(act_l[:, 4 * g:4 * g + 4, cols],
                                      bank[(TURN, VALUE)[g]][:, :].rearrange("p (k c) -> p k c", c=PART),
                                      f32(act_h[:, 4 * g:4 * g + 4, cols]), ALU.subtract)\
                       .then_inc(vector_done, V[stage].step((f"turn{g}", lab)))

            with dve.Fori(0, 3) as t:
                for e in range(2):
                    if e == 0:
                        done = [(T["res"].at((f"m{n}", 1), t, back=1), T["res0"].at(f"m{n}")) for n in range(2)]
                    else:
                        done = [(T["res"].at((f"m{n}", 0), t),) for n in range(2)]
                    residual("res", e, t, e, t * 32 + 16 * (e + 1), *done)
                    merged_lo("res", ("ms", e), e, merged[:, bass.ds(t * 2 + (e + 2), 1), :]
                              .rearrange("p o c -> p (o c)"), t)
                    norm("res", e, t, e)
                    turned_lo("res", e, t, t * 2 + e)
            residual("res7", 0, 0, 0, 16 * 7, (T["res"].at(("m0", 1), 2),), (T["res"].at(("m1", 1), 2),))
            norm("res7", 0, 0, 0)
            turned_lo("res7", 0, 0, 6)
            residual("res7", "t", 0, 1, 16 * 8, (T["res7"].at(("m0", 0)),), (T["res7"].at(("m1", 0)),))
            norm("res7", "t", 0, 1)
            turned_lo("res7", "t", 0, 7)

            def ff(t, last):
                st = V["ff"]
                for s in range(2):
                    split_lo("ff", t, 2 * s + 1, w_h[1][:, :, :], w_l[1][:, :, :])
                    if s == 0:
                        split_lo("ff", t, 2, w_h[0][:, :, :], w_l[0][:, :, :])
                    else:
                        for d in range(2):
                            split_lo("ff", t, 4 + d, wd_h[d][:, :].rearrange("p (k c) -> p k c", c=PART),
                                     wd_l[d][:, :].rearrange("p (k c) -> p k c", c=PART))
                    for half in range(2):
                        cols = slice(HALF * half, HALF * half + HALF)
                        dve.wait_ge(scalar_done, S["ff"].at(("silu", s, half), t))
                        if half == 0:
                            dve.wait_ge(tensor_done, T["ff"].at(("half", 2 * s + 1), t))
                        else:
                            dve.wait_ge(units_done, unit("ff", t, 2 * s + 1) + 1 + BUFFERS)
                        dve.tensor_tensor(silu[:, cols], bank[2 + half][:, :], silu[:, cols], ALU.mult)\
                           .then_inc(vector_done, st.step(("up", s, half)))
                        dve.wait_ge(scalar_done, S["ff"].at(("hi", s, half), t))
                        dve.tensor_tensor(h_l[s][:, cols], silu[:, cols], f32(h_h[s][:, cols]), ALU.subtract)\
                           .then_inc(vector_done, st.step(("lo", s, half)))
                if not last:
                    split_lo("ff", t, 6, w_h[0][:, :, :], w_l[0][:, :, :])
                for tile in range(TILES):
                    for half in range(2):
                        part = y_acc[:, tile, HALF * half:HALF * half + HALF]
                        b = bank[(4, 0)[tile // 2 % 2] + 2 * (tile % 2) + half]
                        dve.wait_ge(tensor_done, T["ff"].at(("down", tile, half), t))
                        dve.tensor_tensor(part, b[:, :], part, ALU.add)\
                           .then_inc(vector_done, st.step(("acc", tile, half)))

            with dve.Fori(0, FF_TRIPS - 1) as t:
                ff(t, False)
            ff(FF_TRIPS - 1, True)
            dve.wait_ge(ln2_landed, 32)
            for t in range(TILES):
                dve.wait_ge(vector_done, V["ff"].end if t == 0 else V["end"].at(("b", t - 1)))
                layer_norm("end", t, 0, y_acc[:, t, :], ln2_gain, ln2_shift)

        @block.tensor
        def _(pe):
            pe.sem_inc(tensor_done, AHEAD)
            pe.sem_inc(units_done, BUFFERS)

            def three(out_ap, stat, mov, start, stop):
                pairs = ((stat[0], mov[0]), (stat[0], mov[1]), (stat[1], mov[0]))
                for n, (lhs, rhs) in enumerate(pairs):
                    ins = pe.matmul(out_ap, lhs, rhs, start=start and n == 0, stop=stop and n == 2)
                return ins

            def one(b, slot, k, half, n, a_h, a_l, start, stop, row=None):
                row = k if row is None else row
                cols = slice(HALF * half, HALF * half + HALF)
                lhs = (w_h[slot], w_h[slot], w_l[slot])[n][:, k, :]
                rhs = (a_h, a_l, a_h)[n][:, row, cols]
                return pe.matmul(b[:, :], lhs, rhs, start=start, stop=stop)

            def turn(b, blocks):
                for n, src in enumerate(blocks):
                    ins = pe.transpose(b[:, PART * n:PART * n + PART], src, ident[:, :])
                return ins

            st = T["x"]
            pe.wait_ge(const_made, 2)
            with pe.Fori(0, X_TRIPS) as t:
                for j in range(X_PER):
                    pe.wait_ge(x_landed[j], t * 16 + 16)
                    for hh in range(2):
                        before = ("x", j - 2, hh) if j >= 2 else ("x", j + 2, hh)
                        pe.wait_ge(vector_done, V["x"].at(before, t, back=int(j < 2)))
                        turn(bank[2 * (j % 2) + hh], [x_in[j][:, PART * k:PART * k + PART]
                                                      for k in range(4 * hh, 4 * hh + 4)])\
                            .then_inc(tensor_done, st.step(("x", j, hh)))

            st = T["heads"]
            v = V["heads"]
            with pe.Fori(0, B_HEADS) as h:
                for s in HEADS:
                    k, a = s[0], s[1:]
                    if k == "mm":
                        n, lo, hi = a
                        for idx in range(lo, hi):
                            half, r = divmod(idx, 24)
                            kt, p = divmod(r, 3)
                            b = bank[2 * (n % 2) + half]
                            if idx == 0:
                                pe.wait_ge(weights_ready, item("heads", h, n) + 1 + BUFFERS)
                            if r == 0:
                                if n == 0:
                                    pe.wait_ge(vector_done, v.at(("out", 4, half), h, back=1))
                                    pe.wait_ge(vector_done, V["x"].at(("x", 3, 1), half))
                                elif n == 1:
                                    pe.wait_ge(vector_done, v.at(("gate", half), h, back=1))
                                elif n in (2, 3):
                                    pe.wait_ge(vector_done, v.at(("out", n - 2, half), h))
                                else:
                                    pe.wait_ge(scalar_done, S["heads"].at(("out", n - 2, half), h))
                            ins = one(b, n % 2, kt, half, p, act_h, act_l, r == 0, r == 23)
                            if idx == 23:
                                ins.then_inc(tensor_done, st.step(("half", n)))
                            elif idx == 47:
                                ins.then_inc(units_done, 1)
                    elif k == "scores":
                        i, c = a
                        keys = min(HALF, PART * (i + 1) - HALF * c)
                        if i == 0:
                            pe.wait_ge(vector_done, v.at(("out", 1, 1), h))
                        else:
                            before = (i, 0) if c else (i - 1, int(i - 1 >= 4))
                            pe.wait_ge(vector_done, v.at(("logit", *before, 1), h))
                        for p in range(3):
                            for m in range(2):
                                rows = slice(HEAD * m, HEAD * m + HEAD)
                                q = (q_h, q_h, q_l)[p][rows, PART * i:PART * i + PART]
                                kk = (k_h, k_l, k_h)[p][rows, HALF * c:HALF * c + keys]
                                ins = pe.matmul(bank[SCORES[m]][:, 0:keys], q, kk, start=p == 0, stop=p == 2)
                        ins.then_inc(tensor_done, st.step(s))
                    elif k == "turn":
                        i, g = a
                        n = min(4, i + 1 - 4 * g)
                        if g == 0:
                            pe.wait_ge(vector_done, v.at(("mix", i), h))
                        before = (("turn", i, 0) if g else
                                  ("vturn", 0) if i == 0 else ("turn", i - 1, int(i - 1 >= 4)))
                        pe.wait_ge(vector_done, v.at(before, h))
                        turn(bank[TURN], [prob[i % 2][0][:, PART * j:PART * j + PART]
                                          for j in range(4 * g, 4 * g + n)]).then_inc(tensor_done, st.step(s))
                    elif k == "vturn":
                        g = a[0]
                        pe.wait_ge(scalar_done, S["heads"].at(("out", 2, g), h))
                        pe.wait_ge(vector_done, v.at(("yturn", g), h, back=1))
                        turn(bank[(TURN, VALUE)[g]], [v_t[:, PART * j:PART * j + PART]
                                                      for j in range(4 * g, 4 * g + 4)])\
                            .then_inc(tensor_done, st.step(s))
                    elif k == "value":
                        i = a[0]
                        pe.wait_ge(vector_done, v.at(("turn", i, int(i >= 4)), h))
                        pe.wait_ge(vector_done, v.at(("sum", i - 1) if i else ("vturn", 1), h))
                        for j in range(i + 1):
                            pe.matmul(bank[VALUE][:, 0:2 * PART], wt_h[:, j, :], v_hl[:, j, :], start=j == 0, stop=False)
                            ins = pe.matmul(bank[VALUE][:, 0:PART], wt_l[:, j, :], v_hl[:, j, 0:PART], start=False,
                                            stop=j == i)
                        ins.then_inc(tensor_done, st.step(s))
                    elif k == "yturn":
                        g = a[0]
                        if g == 0:
                            pe.wait_ge(vector_done, v.at(("rmul",), h))
                        turn(bank[(TURN, VALUE)[g]], [mixed[:, j, :] for j in range(4 * g, 4 * g + 4)])\
                            .then_inc(tensor_done, st.step(s))

            st = T["proj"]
            pe.wait_ge(vector_done, V["heads"].end)
            with pe.Fori(0, A_UNITS // 2) as t:
                for e in range(2):
                    pe.wait_ge(weights_ready, item("proj", t, e) + 1 + BUFFERS)
                    for half in range(2):
                        pe.wait_ge(scalar_done, S["proj"].at(("out", e, half), t, back=1))
                        for idx in range(24):
                            kt, p = divmod(idx, 3)
                            ins = one(bank[2 * e + half], e, kt, half, p, act_h, act_l, idx == 0, idx == 23)
                        if half == 0:
                            ins.then_inc(tensor_done, st.step(("half", e)))
                        else:
                            ins.then_inc(units_done, 1)

            st = T["window"]
            v = V["window"]
            pe.wait_ge(scalar_done, S["proj"].end)
            with pe.Fori(0, TILES // 2) as t:
                for s in WIN:
                    k, e, a = s[0], s[1], s[2:]
                    if k == "mm":
                        n, lo, hi = a
                        per = 24 if n < 2 else 12
                        for idx in range(lo, hi):
                            q, r = divmod(idx, per)
                            kt, p = divmod(r, 3)
                            br, half = (n, q) if n < 2 else divmod(q, 2)
                            if idx == 0:
                                pe.wait_ge(weights_ready, item("window", t, 3 * e + n) + 1 + BUFFERS)
                            if r == 0:
                                if n < 2:
                                    pe.wait_ge(vector_done, v.at(("out", 1 - e, 2, 2 * n + half), t, back=1 - e))
                                else:
                                    pe.wait_ge(scalar_done, S["window"].at(("out", e, br, half), t))
                            b = bank[2 * br + half]
                            slot = (3 * e + n) % 2
                            if n < 2:
                                ins = one(b, slot, kt, half, p, act_h, act_l, r == 0, r == per - 1)
                            else:
                                y = ((yb_h, yb_l), (yc_h, yc_l))[br]
                                ins = one(b, slot, BRANCH_KT * br + kt, half, p, *y, r == 0, r == per - 1, row=kt)
                            if idx == 47:
                                ins.then_inc(units_done, 1)
                            elif r == per - 1:
                                ins.then_inc(tensor_done, st.step(("part", e, n, idx + 1)))
                    elif k == "vturn":
                        pe.wait_ge(window_landed, t * 128 + 64 * (e + 1))
                        pe.wait_ge(vector_done, v.at(("yturn", 1 - e, 1), t, back=1 - e))
                        turn(bank[TURN], [vf[:, 0:PART], vf[:, PART:2 * PART]]).then_inc(tensor_done, st.step(s))
                    elif k == "scores":
                        g = a[0]
                        pe.wait_ge(vector_done, v.at(("qsplit", e, g), t))
                        if g:
                            pe.wait_ge(vector_done, v.at(("logit", e, 0, 3), t))
                        for pair in range(2):
                            for p in range(3):
                                for r in range(2):
                                    rows = slice(HEAD * r, HEAD * r + HEAD)
                                    q = (qs_h, qs_h, qs_l)[p][rows, pair, :]
                                    kk = (ks_h, ks_l, ks_h)[p][rows, g, :]
                                    ins = pe.matmul(bank[SCORES[r]][:, WINDOW * pair:WINDOW * pair + WINDOW], q, kk,
                                                    start=p == 0, stop=p == 2)
                        ins.then_inc(tensor_done, st.step(s))
                    elif k == "turn":
                        g, pair = a
                        pe.wait_ge(scalar_done, S["window"].at(("exp", e, g, 2 * pair + 1), t))
                        before = {(0, 0): ("vturn", e), (0, 1): ("turn", e, 0, 0), (1, 0): ("turn", e, 0, 1),
                                  (1, 1): ("yturn", e, 0)}[g, pair]
                        pe.wait_ge(vector_done, v.at(before, t))
                        turn(bank[TURN], [a_prob[g][:, 2 * pair + n, PART * blk:PART * blk + PART]
                                          for n in range(2) for blk in range(2)]).then_inc(tensor_done, st.step(s))
                    elif k == "value":
                        g, pair = a
                        pe.wait_ge(vector_done, v.at(("turn", e, g, pair), t))
                        if pair == 0:
                            pe.wait_ge(vector_done, v.at(("sum", e, 0), t) if g else
                                       v.at(("sum", 1 - e, 1), t, back=1 - e))
                        for n in range(2):
                            c = 2 * HEAD * (2 * pair + n)
                            for blk in range(2):
                                pe.matmul(bank[VALUE][:, c:c + 2 * HEAD], at_h[:, 2 * n + blk, :], vs_hl[:, blk, g, :],
                                          start=blk == 0, stop=False)
                                ins = pe.matmul(bank[VALUE][:, c:c + HEAD], at_l[:, 2 * n + blk, :],
                                                vs_hl[:, blk, g, 0:HEAD], start=False, stop=blk == 1)
                        ins.then_inc(tensor_done, st.step(s))
                    elif k == "yturn":
                        g = a[0]
                        pe.wait_ge(vector_done, v.at(("norm", e, g), t))
                        pe.wait_ge(vector_done, v.at(("turn", e, 1, g), t))
                        turn(bank[TURN], [a_mix[:, 2 * n:2 * n + 2, :].rearrange("p a c -> p (a c)")
                                          for n in range(2)]).then_inc(tensor_done, st.step(s))

            st = T["merge"]
            pe.wait_ge(vector_done, V["window"].end)
            with pe.Fori(0, KT // 2) as t:
                for e in range(2):
                    for n in range(2):
                        kts = (KT, BRANCH_KT)[n]
                        pe.wait_ge(weights_ready, item("merge", t, 3 * e + n) + 1 + BUFFERS)
                        for half in range(2):
                            if n == 0:
                                pe.wait_ge(scalar_done, S["merge"].at(("out", 1 - e, half), t, back=1 - e))
                            else:
                                pe.wait_ge(vector_done, V["merge"].at(("mul", 1 - e, half), t, back=1 - e))
                            for idx in range(3 * kts):
                                kt, p = divmod(idx, 3)
                                a_h, a_l = ((act_h, act_l), (ya_h, ya_l))[n]
                                ins = one(bank[2 * n + half], n, kt, half, p, a_h, a_l, idx == 0, idx == 3 * kts - 1)
                            if half == 0:
                                ins.then_inc(tensor_done, st.step(("part", e, n)))
                            else:
                                ins.then_inc(units_done, 1)

            def project(slot, stage, labels):
                for half in range(2):
                    cols = slice(HALF * half, HALF * half + HALF)
                    for kt in range(KT):
                        ins = three(bank[2 * slot + half][:, :], (m_h[slot][:, kt, :], m_l[slot][:, kt, :]),
                                    (wo_h[:, kt, cols], wo_l[:, kt, cols]), kt == 0, kt == KT - 1)
                    ins.then_inc(tensor_done, T[stage].step(labels[half]))

            def turn_normed(stage, lab, trip, slot, before):
                pe.wait_ge(vector_done, V[stage].at(("b", lab), trip))
                for g in range(2):
                    pe.wait_ge(vector_done, before[g])
                    turn(bank[(TURN, VALUE)[g]], [normed[slot][:, PART * k:PART * k + PART]
                                                  for k in range(4 * g, 4 * g + 4)])\
                        .then_inc(tensor_done, T[stage].step((f"turn{g}", lab)))

            pe.wait_ge(weights_ready, item("merge", KT // 2, 0) + BUFFERS)
            pe.wait_ge(vector_done, V["res0"].at("ms0"))
            project(0, "res0", ("m0", "m1"))
            with pe.Fori(0, 3) as t:
                for e in range(2):
                    slot = 1 - e
                    if e == 0:
                        pe.wait_ge(vector_done, V["res"].at(("ms", 1), t, back=1))
                        pe.wait_ge(vector_done, V["res0"].at("ms1"))
                    else:
                        pe.wait_ge(vector_done, V["res"].at(("ms", 0), t))
                    project(slot, "res", (("m0", e), ("m1", e)))
                    turn_normed("res", e, t, e, [V["res"].at((f"turn{g}", 1 - e), t, back=1 - e) for g in range(2)])
            pe.wait_ge(vector_done, V["res"].at(("ms", 1), 2))
            project(1, "res7", (("m0", 0), ("m1", 0)))
            turn_normed("res7", 0, 0, 0, [V["res"].at((f"turn{g}", 1), 2) for g in range(2)])
            turn_normed("res7", "t", 0, 1, [V["res7"].at((f"turn{g}", 0)) for g in range(2)])

            st = T["ff"]
            v = V["ff"]
            pe.wait_ge(vector_done, V["res7"].end)

            def ff(t):
                for n in range(4):
                    pe.wait_ge(weights_ready, item("ff", t, n) + 1 + BUFFERS)
                    for half in range(2):
                        if n < 2:
                            pe.wait_ge(vector_done, v.at(("acc", 6 + n, half), t, back=1))
                        elif n == 2:
                            pe.wait_ge(scalar_done, S["ff"].at(("silu", 0, half), t))
                        else:
                            pe.wait_ge(vector_done, v.at(("up", 0, half), t))
                        for idx in range(24):
                            kt, p = divmod(idx, 3)
                            ins = one(bank[2 * (n % 2) + half], n % 2, kt, half, p, act_h, act_l, idx == 0, idx == 23)
                        if half == 0:
                            ins.then_inc(tensor_done, st.step(("half", n)))
                        else:
                            ins.then_inc(units_done, 1)
                pe.wait_ge(weights_ready, item("ff", t, 5) + 1 + BUFFERS)
                for quad in range(TILES // 2):
                    for s in range(2):
                        if quad == 0 and s == 1:
                            pe.wait_ge(vector_done, v.at(("lo", 1, 1), t))
                        for tile in (2 * quad, 2 * quad + 1):
                            for half in range(2):
                                n = 2 * (tile % 2) + half
                                b = bank[(4, 0)[quad % 2] + n]
                                if s == 0:
                                    if quad == 0:
                                        pe.wait_ge(vector_done, v.at(("acc", 4 + tile, half), t, back=1))
                                    elif quad == 1:
                                        pe.wait_ge(vector_done, v.at(("up", 1, half), t))
                                        pe.wait_ge(scalar_done, S["ff"].at(("silu", 1, half), t))
                                    else:
                                        pe.wait_ge(vector_done, v.at(("acc", tile - 4, half), t))
                                rows = slice(PART * tile, PART * tile + PART)
                                cols = slice(HALF * half, HALF * half + HALF)
                                ins = three(b[:, :], (h_h[s][:, rows], h_l[s][:, rows]),
                                            (wd_h[s][:, cols], wd_l[s][:, cols]), s == 0, s == 1)
                                if s == 1:
                                    ins.then_inc(tensor_done, st.step(("down", tile, half)))

            with pe.Fori(0, FF_TRIPS - 1) as t:
                ff(t)
            ff(FF_TRIPS - 1)


_INS = ["x", "w_in", "sink", "lam_q1", "lam_k1", "lam_q2", "lam_k2", "subln_g", "conv_w", "w_branch", "w_gate", "b_gate",
        "w_out", "ln1_g", "ln1_b", "w_ffn_in", "w_ffn_down", "ln2_g", "ln2_b"]


def kernel(**inputs):
    import numpy as np
    import concourse.bacc as bacc
    from concourse.bass_utils import run_bass_kernel_spmd

    nc = bacc.Bacc("TRN2", target_bir_lowering=False, num_devices=1, dynamic_dma_scratch_size=1024)
    arrays, args = {}, []
    for name in _INS:
        a = np.ascontiguousarray(inputs[name])
        arrays[f"in_{name}"] = a
        args.append(nc.dram_tensor(f"in_{name}", a.shape, mybir.dt.from_np(a.dtype), kind="ExternalInput").ap())
    shape = inputs["x"].shape
    args.append(nc.dram_tensor("out_dram", shape, F32, kind="ExternalOutput").ap())
    hybrid_encoder_layer(nc, *args)
    r = run_bass_kernel_spmd(nc, [arrays], core_ids=[0])
    return r.results[0]["out_dram"]
```

```python
import math

import concourse.bass as bass
from concourse import mybir
from concourse.alu_op_type import AluOpType as ALU
from contextlib import ExitStack

F32 = mybir.dt.float32
F32R = mybir.dt.float32r
BF16 = mybir.dt.bfloat16
ACT = mybir.ActivationFunctionType

PART = 128
HALF = 512
TOKENS = 1024
WIDTH = 1024
KT = WIDTH // PART
TILES = TOKENS // PART
CHUNK = 64
HEAD = 64
A_HEADS = 8
A_GROUP = 4
B_HEADS = 4
C_TILES = 4
BRANCH_KT = 4
WINDOW = 192
D_FF = 2816
FF_PAIRS = D_FF // PART
FF_TRIPS = FF_PAIRS // 2
ALPHA = 2.0 ** 0.25
EPS = 1e-5
LAMBDA_INIT = 0.8 - 0.6 * math.exp(-0.3 * 0)
Q_SCALE = -(HEAD ** -0.5)
RMS_SHIFT = 2.0 ** -20
MASKED = 1e32

COL_QB = (A_HEADS + 4) * HEAD
COL_KB = COL_QB + B_HEADS * PART
COL_VB = COL_KB + B_HEADS * PART
COL_CB = COL_VB + B_HEADS * PART
COL_CC = COL_CB + C_TILES * PART
COL_CU = COL_CC + C_TILES * PART
A_UNITS = COL_QB // PART

SCORES = (4, 5)
TURN = 6
VALUE = 7

AHEAD = 256
BUFFERS = 2


class Stage:

    def __init__(self, start, labels, trips=1):
        self.start, self.labels, self.trips = start, labels, trips
        self.place = {label: n for n, label in enumerate(labels)}
        assert len(self.place) == len(labels)
        self.said = 0

    @property
    def end(self):
        return self.start + len(self.labels) * self.trips

    def at(self, label, trip=0, back=0):
        n = self.start + self.place[label] + 1 - back * len(self.labels)
        return trip * len(self.labels) + n

    def step(self, label):
        assert self.labels[self.said % len(self.labels)] == label, (label, self.labels[self.said % len(self.labels)])
        self.said += 1
        return 1


def heads_script():
    atoms = [(0, [("decay",)]), (106, [("scores", 0, 0), ("exps", 0)]), (126, [("scores", 1, 0), ("exps", 1)]),
             (152, [("vturn", 0), ("vturn", 1)])]
    at = 156
    for i in range(2, 8):
        if i == 2:
            atoms.append((at, [("mix", 0)]))
        atoms.append((at + 2, [("turn", i - 2, 0)]))
        if i >= 4:
            atoms.append((at + 4, [("scores", i, 0)]))
        if i >= 6:
            atoms.append((at + 6, [("turn", i - 2, 1)]))
        atoms.append((at + 10, [("value", i - 2), ("mix", i - 1), ("scores", i, int(i >= 4))]
                      + ([("exps", i)] if i < 7 else [])))
        at += 13
    atoms += [(at + 1, [("turn", 6, 0)]), (at + 6, [("turn", 6, 1), ("exps", 7)]), (at + 12, [("value", 6)]),
              (at + 13, [("mix", 7), ("conv",)]), (at + 26, [("turn", 7, 0)]), (at + 30, [("turn", 7, 1)]),
              (at + 34, [("value", 7), ("rms",)])]
    atoms.append((286, [("yturn", 0), ("yturn", 1)]))
    script, at = [], 0

    def dense(upto):
        nonlocal at
        while at < upto:
            n, a = divmod(at, 48)
            if a == 0:
                script.append(("split", n + 1))
            b = min(upto - 48 * n, 24 if a < 24 else 48)
            script.append(("mm", n, a, b))
            if b in (24, 48) and n < 5:
                script.append(("out", n, b // 24 - 1))
            at = 48 * n + b

    for upto, steps in atoms:
        dense(upto)
        script.extend(steps)
    dense(48 * 6)
    return script + [("out", 5, 0), ("out", 5, 1)]


def heads_labels(script):
    vec, sca, ten = [], [], []
    for s in script:
        k, a = s[0], s[1:]
        if k == "decay":
            vec.append(s)
        elif k == "mm" and a[2] == 24:
            ten.append(("half", a[0]))
        elif k == "out":
            if a[0] in (0, 1, 2, 3, 5):
                sca.append(s)
            if a[0] == 5:
                vec.append(("gate", a[1]))
            if a[0] in (0, 1, 4, 5):
                vec.append(s)
        elif k == "conv":
            vec += [("conv", n) for n in range(3)]
        elif k == "scores":
            ten.append(s)
            vec += [("logit", *a, 0), ("logit", *a, 1)]
            if a[1] == 1:
                vec.append(("peak", a[0]))
        elif k == "exps":
            sca += [("exp", a[0], 0), ("exp", a[0], 1)]
        elif k == "mix":
            vec += [("inv", *a), ("coef", *a), ("mix", *a)]
        elif k in ("turn", "vturn", "yturn"):
            ten.append(s)
            sca.append(s)
            if k == "yturn":
                vec.append(s)
        elif k == "value":
            ten.append(s)
            sca += [("out", "value", *a), ("square", *a)]
        elif k == "rms":
            sca.append(("root",))
            vec += [("rinv",), ("rscale",), ("rmul",)]
    return vec, sca, ten


def window_script():
    atoms = [(32, [("vturn",)]), (34, [("scores", 0)]), (42, [("scores", 1)]), (58, [("turn", 0, 0)]),
             (66, [("turn", 0, 1)]), (68, [("value", 0, 0)]), (74, [("turn", 1, 0)]), (77, [("value", 0, 1)]),
             (82, [("turn", 1, 1), ("unmask",)]), (85, [("value", 1, 0)]), (92, [("value", 1, 1), ("norm",)]),
             (105, [("yturn",)])]
    script = []
    for e in range(2):
        at = 0

        def dense(upto):
            nonlocal at
            while at < upto:
                n, a = divmod(at, 48)
                if a == 0:
                    script.append(("split", 3 * e + n + 1))
                step = 24 if n < 2 else 12
                b = min(upto - 48 * n, (a // step + 1) * step)
                script.append(("mm", e, n, a, b))
                if b % step == 0:
                    script.append(("out", e, n, b // step - 1))
                at = 48 * n + b

        for upto, steps in atoms:
            dense(upto)
            script.extend((s[0], e, *s[1:]) for s in steps)
        dense(48 * 3)
        script += [("add", e), ("store", e)]
    return script


def window_labels(script):
    vec, sca, ten = [], [], []
    for s in script:
        k, a = s[0], s[1:]
        if k == "mm" and ((a[1] < 2 and a[3] == 24) or (a[1] == 2 and a[3] in (12, 24, 36))):
            ten.append(("part", a[0], a[1], a[3]))
        elif k == "out":
            (sca if a[1] < 2 else vec).append(s)
        elif k in ("turn", "vturn", "yturn"):
            ten.append(s)
            sca.append(s)
            if k == "yturn":
                vec.append(s)
        elif k == "scores":
            ten.append(s)
            vec += [("logit", *a, n) for n in range(A_GROUP)]
            sca += [("exp", *a, n) for n in range(A_GROUP)]
            vec.append(("sub", *a))
            sca.append(("sink", *a))
        elif k == "value":
            ten.append(s)
        elif k == "norm":
            vec += [("den", *a), ("inv", *a), ("norm", *a)]
        elif k in ("unmask", "add"):
            vec.append(s)
    return vec, sca, ten


def hybrid_encoder_layer(nc, x, w_in, sink, lam_q1, lam_k1, lam_q2, lam_k2, subln_g, conv_w, w_branch, w_gate,
                         b_gate, w_out, ln1_g, ln1_b, w_ffn_in, w_ffn_down, ln2_g, ln2_b, out):
    x_tiles = x[0].rearrange("(t p) d -> t p d", p=PART)
    out_tiles = out[0].rearrange("(t p) d -> t p d", p=PART)
    w_in_k = w_in[0].rearrange("(k p) c -> p k c", p=PART)
    w_gate_k = w_gate[0].rearrange("(k p) c -> p k c", p=PART)
    w_branch_k = w_branch[0].rearrange("n (k p) c -> p (n k) c", p=PART)
    w_out_k = w_out[0].rearrange("(k p) c -> p k c", p=PART)
    w_ffn_k = w_ffn_in[0].rearrange("(k p) c -> p k c", p=PART)
    w_down_k = w_ffn_down[0].rearrange("(k p) c -> k p c", p=PART)

    window_proj = nc.dram_tensor("window_proj", [A_UNITS, PART, PART + TOKENS], F32).ap()
    merged_bc = nc.dram_tensor("merged_bc", [KT, PART, TOKENS], F32).ap()

    ctx = ExitStack()
    with ctx:
        place = [1152]

        def put(name, shape, dt=F32, at=None):
            size = 2 if dt == BF16 else 4
            for n in shape[1:]:
                size *= n
            where = place[0] if at is None else at[0]
            t = nc.alloc_sbuf_tensor_at(name, shape, dt, offset=where)
            assert where + size <= 229344, (name, where + size)
            where = (where + size + 31) // 32 * 32
            if at is None:
                place[0] = where
            else:
                at[0] = where
            return t

        def sem(name):
            return ctx.enter_context(nc.semaphore(name))

        act_h = put("act_h", [PART, KT, TOKENS], F32R)
        act_l = put("act_l", [PART, KT, TOKENS], F32R)
        raw = [put(f"raw{n}", [PART, KT, PART]) for n in range(BUFFERS)]
        w_h = [put(f"w_h{n}", [PART, KT, PART], F32R) for n in range(BUFFERS)]
        w_l = [put(f"w_l{n}", [PART, KT, PART], F32R) for n in range(BUFFERS)]
        ident = put("ident", [PART, PART])
        gate_bias = put("gate_bias", [PART, 3 * KT])
        conv_taps = put("conv_taps", [PART, C_TILES, 3])
        rms_gain = put("rms_gain", [PART, 1])
        neg_sink = put("neg_sink", [PART, A_HEADS])
        neg_lam = put("neg_lam", [PART, 1])
        rms_eps = put("rms_eps", [PART, 1])
        ln_eps = put("ln_eps", [PART, 1])
        low = put("low", [PART, TILES, 2, 2])
        den = put("den", [PART, TILES, 2])
        inv = put("inv", [PART, TILES, 2])
        coef = put("coef", [PART, TILES])
        square_sum = put("square_sum", [PART, TILES])
        proj_scale = put("proj_scale", [PART, A_UNITS])
        rms_root = put("rms_root", [PART, TILES])
        rms_inv = put("rms_inv", [PART, TILES])
        a_low = put("a_low", [PART, A_HEADS])
        a_den = put("a_den", [PART, A_HEADS])
        a_sink = put("a_sink", [PART, A_HEADS])
        a_sunk = put("a_sunk", [PART, A_HEADS])
        a_inv = put("a_inv", [PART, A_HEADS])
        stats = put("stats", [PART, 2, 6])
        moments = put("moments", [PART, 2])
        ln_root = put("ln_root", [PART, 1])
        ln_inv = put("ln_inv", [PART, 1])
        base = place[0]
        KB = 1024

        at = [base]
        yb_h = put("yb_h", [PART, B_HEADS, TOKENS], F32R, at)
        yb_l = put("yb_l", [PART, B_HEADS, TOKENS], F32R, at)
        yc_h = put("yc_h", [PART, C_TILES, TOKENS], F32R, at)
        yc_l = put("yc_l", [PART, C_TILES, TOKENS], F32R, at)
        behind_y = at[0]
        q_h = put("q_h", [PART, TOKENS], F32R, at)
        q_l = put("q_l", [PART, TOKENS], F32R, at)
        k_h = put("k_h", [PART, TOKENS], F32R, at)
        k_l = put("k_l", [PART, TOKENS], F32R, at)
        v_b = put("v_b", [PART, TILES, PART], F32, at)
        prob = [[put(f"prob{n}{m}", [PART, TOKENS], F32, at) for m in range(2)] for n in range(3)]
        bias_b = put("bias_b", [PART, TOKENS], F32, at)
        weights_t = put("weights_t", [PART, TILES, PART], F32, at)
        mixed = put("mixed", [PART, TILES, PART], F32, at)
        v_t = put("v_t", [PART, TOKENS], F32, at)
        conv = put("conv", [PART, TOKENS], F32, at)
        gated = put("gated", [PART, 2 + TOKENS], F32, at)
        squares = put("squares", [PART, PART], F32, at)
        at = [base]
        x_in = [put(f"x_in{n}", [PART, WIDTH], F32, at) for n in range(TILES)]
        lam_in = put("lam_in", [PART, 4, HEAD], F32, at)
        lam_out = put("lam_out", [PART, 2, HEAD], F32, at)
        lam_sum = put("lam_sum", [PART, 2], F32, at)
        lam_exp = put("lam_exp", [PART, 2], F32, at)
        sink_in = put("sink_in", [PART, A_HEADS], F32, at)
        gain_in = put("gain_in", [PART, 1], F32, at)
        zeros = put("zeros", [PART, PART], F32, at)
        ramp_b = put("ramp_b", [PART, TOKENS], F32, at)
        at = [behind_y]
        ya_h = put("ya_h", [PART, BRANCH_KT, TOKENS], F32R, at)
        ya_l = put("ya_l", [PART, BRANCH_KT, TOKENS], F32R, at)
        behind_ya = at[0]
        at = [behind_y]
        to_dram = [put(f"to_dram{n}", [PART, TOKENS], F32, at) for n in range(2)]
        ramp_a = put("ramp_a", [PART, WINDOW], F32, at)
        ramp_abs = put("ramp_abs", [PART, WINDOW], F32, at)
        at = [behind_ya]
        bias_a = put("bias_a", [PART, A_HEADS, WINDOW], BF16, at)
        near_a = put("near_a", [PART, A_HEADS, CHUNK], BF16, at)
        sig_b = put("sig_b", [PART, TOKENS], F32, at)
        sig_c = put("sig_c", [PART, TOKENS], F32, at)
        qf = [put(f"qf{n}", [PART, 4, PART], F32, at) for n in range(2)]
        kf = [put(f"kf{n}", [PART, 2, WINDOW], F32, at) for n in range(2)]
        vf = [put(f"vf{n}", [PART, 2 * PART], F32, at) for n in range(2)]
        v_a = put("v_a", [PART, 2, 2, HEAD], F32, at)
        a_prob = [put(f"a_prob{g}", [PART, A_GROUP, 2 * PART], F32, at) for g in range(2)]
        a_turned = [put(f"a_turned{n}", [PART, 4, PART], F32, at) for n in range(2)]
        a_mix = put("a_mix", [PART, A_HEADS, HEAD], F32, at)
        at = [base]
        wo_h = put("wo_h", [PART, KT, WIDTH], F32R, at)
        wo_l = put("wo_l", [PART, KT, WIDTH], F32R, at)
        at = [behind_ya]
        merged = put("merged", [PART, TILES, WIDTH], F32, at)
        sig_a = put("sig_a", [PART, TOKENS], F32, at)
        at = [behind_y]
        m_h = [put(f"m_h{n}", [PART, KT, PART], F32R, at) for n in range(2)]
        m_l = [put(f"m_l{n}", [PART, KT, PART], F32R, at) for n in range(2)]
        normed = [put(f"normed{n}", [PART, WIDTH], F32, at) for n in range(2)]
        x_res = put("x_res", [PART, WIDTH], F32, at)
        ln_shift = put("ln_shift", [PART, WIDTH], F32, at)
        assert at[0] <= behind_ya
        at = [behind_ya + 32 * KB]
        ln_gain = put("ln_gain", [PART, WIDTH], F32, at)
        at = [base]
        h_h = [put(f"h_h{n}", [PART, TOKENS], F32R, at) for n in range(4)]
        h_l = [put(f"h_l{n}", [PART, TOKENS], F32R, at) for n in range(4)]
        wd_h = [put(f"wd_h{n}", [PART, WIDTH], F32R, at) for n in range(4)]
        wd_l = [put(f"wd_l{n}", [PART, WIDTH], F32R, at) for n in range(4)]
        silu = put("silu", [PART, TOKENS], F32, at)
        ln2_gain = put("ln2_gain", [PART, WIDTH], F32, at)
        ln2_shift = put("ln2_shift", [PART, WIDTH], F32, at)
        moments2 = put("moments2", [PART, TILES, 2], F32, at)
        root2 = put("root2", [PART, TILES], F32, at)
        inv2 = put("inv2", [PART, TILES], F32, at)
        offset2 = put("offset2", [PART, TILES], F32, at)
        assert at[0] <= behind_y + 16 * KB
        y_acc = merged

        bank = [ctx.enter_context(nc.psum_tensor(f"bank{n}", [PART, HALF], F32)) for n in range(8)]

        tensor_done = sem("tensor_done")
        vector_done = sem("vector_done")
        scalar_done = sem("scalar_done")
        units_done = sem("units_done")
        weights_hi = sem("weights_hi")
        weights_ready = sem("weights_ready")
        raw_landed = [sem(f"raw_landed{n}") for n in range(BUFFERS)]
        scores_seen = sem("scores_seen")
        moments_seen = sem("moments_seen")
        gates_seen = sem("gates_seen")
        scales_seen = sem("scales_seen")
        x_landed = [sem(f"x_landed{n}") for n in range(TILES)]
        small_landed = sem("small_landed")
        const_made = sem("const_made")
        zeros_stored = sem("zeros_stored")
        proj_stored = [sem(f"proj_stored{n}") for n in range(2)]
        bias_a_made = sem("bias_a_made")
        window_landed = [sem(f"window_landed{n}") for n in range(2)]
        merged_stored = sem("merged_stored")
        merged_landed = [sem(f"merged_landed{n}") for n in range(2)]
        ln_landed = sem("ln_landed")
        ln2_landed = sem("ln2_landed")
        res_landed = sem("res_landed")
        gained = sem("gained")
        out_stored = sem("out_stored")

        X_FIRST = TILES // 2

        def x_banks(t):
            return t if t < 4 else (t - 4) % 3 + 1

        x_labels = [("x", t, hh) for t in range(TILES) for hh in range(2)]
        HEADS = heads_script()
        hv, hs, ht = heads_labels(HEADS)
        WIN = window_script()
        wv, ws, wt = window_labels(WIN)
        merge_v = [(k, e, h) for e in range(2) for h in range(2) for k in ("mul", "acc")]
        merge_s = [("out", e, h) for e in range(2) for h in range(2)]
        merge_t = [("part", e, n) for e in range(2) for n in range(2)]
        ln_v = ["st0", "st1", "ag", "ri", "z", "g", "b"]
        res0_ms = [("ms", 0, 0), ("ms", 0, 1), ("ms", 1, 0), ("ms", 1, 1)]
        res_v = [(k, e) for e in range(2) for k in ["r0", "r1", "ms", *ln_v, "turn0", "turn1"]]
        res_s = [(k, e) for e in range(2) for k in ("ms", "root", "keep", "turn0", "turn1")]
        res_t = [(k, e) for e in range(2) for k in ("m0", "m1", "turn0", "turn1")]
        last_v = [(k, n) for n in (0, "t") for k in ["r0", "r1", *ln_v, "turn0", "turn1"]]
        last_s = [(k, n) for n in (0, "t") for k in ("root", "keep", "turn0", "turn1")]
        last_t = [("m0", 0), ("m1", 0), ("turn0", 0), ("turn1", 0)]
        ff_v = [(k, s, h) for s in range(2) for h in range(2) for k in ("up", "lo")]
        ff_v += [("acc", t, h) for t in range(TILES) for h in range(2)]
        ff_s = [x for s in range(2) for x in (("silu", s, 0), ("silu", s, 1), ("hi", s, 0), ("hi", s, 1))]
        ff_t = [("half", n) for n in range(4)] + [("down", t, h) for t in range(TILES) for h in range(2)]
        ff_first_t = ff_t[:1] + [("turn0", "t"), ("turn1", "t")] + ff_t[1:]
        end_v = []
        for t in range(TILES + 2):
            if t < TILES:
                end_v += [("acc", t, 0), ("acc", t, 1)] + [(k, t) for k in ("st0", "st1", "ag", "ri", "off")]
            if t >= 2:
                end_v.append(("b", t - 2))
        end_s = [(k, t) for t in range(TILES) for k in ("root", "z")]
        LOOPED = FF_TRIPS - 2

        def chain(parts):
            stages, start = {}, AHEAD
            for name, labels, trips in parts:
                stages[name] = Stage(start, labels, trips)
                start = stages[name].end
            return stages

        init_v = ["l0", "l1", "dl", "nl", "gain", "sink", "ramp"]
        V = chain([("x", x_labels, 1), ("init", init_v, 1), ("heads", hv, B_HEADS), ("window", wv, TILES // 2),
                   ("merge", merge_v, KT // 2), ("res0", res0_ms, 1), ("res", res_v, 3),
                   ("res7", last_v, 1), ("ff", ff_v, LOOPED), ("ff_before_last", ff_v[:8], 1),
                   ("last", ff_v[:8], 1), ("end", end_v, 1)])
        S = chain([("x", x_labels, 1), ("init", ["le"], 1), ("heads", hs, B_HEADS),
                   ("proj", [("out", e, h) for e in range(2) for h in range(2)], A_UNITS // 2),
                   ("window", ws, TILES // 2), ("merge", merge_s, KT // 2), ("res0", res0_ms, 1),
                   ("res", res_s, 3), ("res7", last_s, 1), ("ff", ff_s, FF_TRIPS), ("end", end_s, 1)])
        T = chain([("x", x_labels, 1), ("heads", ht, B_HEADS),
                   ("proj", [("half", e) for e in range(2)], A_UNITS // 2), ("window", wt, TILES // 2),
                   ("merge", merge_t, KT // 2), ("res0", ["m0", "m1"], 1), ("res", res_t, 3), ("res7", last_t, 1),
                   ("ff_first", ff_first_t, 1)])
        T["ff"] = Stage(T["ff_first"].end - len(ff_t), ff_t, LOOPED)
        T["ff_before_last"] = Stage(T["ff"].end, ff_t[:4])
        T["last"] = Stage(T["ff_before_last"].end, ff_t)

        def of(stages, t):
            if not isinstance(t, int):
                return stages["ff"], t
            if t == 0:
                return stages.get("ff_first", stages["ff"]), 0
            return {LOOPED: (stages.get("ff_before_last", stages["ff"]), 0 if "ff_before_last" in stages else t),
                    LOOPED + 1: (stages.get("last", stages["ff"]), 0 if "last" in stages else t)}[t]

        def in_ff(stages, label, t, back=0):
            if not back:
                stage, trip = of(stages, t)
                return stage.at(label, trip)
            if not isinstance(t, int) or t <= LOOPED:
                return stages["ff"].at(label, t, back=1)
            return of(stages, t - 1)[0].at(label, of(stages, t - 1)[1])

        def down_slots(t):
            return (2, 3) if isinstance(t, int) and t == LOOPED + 1 else (0, 1)

        ITEMS = {"heads": 0, "proj": 24, "window": 30, "merge": 54, "ff": 78}
        UNITS = {"heads": 0, "proj": 24, "window": 30, "merge": 54, "ff": 70}

        def item(stage, trip, n):
            per = {"heads": 6, "proj": 2, "window": 6, "merge": 6, "ff": 6}[stage]
            return trip * per + (ITEMS[stage] + n)

        def landed(stage, trip, n):
            per = {"heads": 6, "proj": 2, "window": 6, "merge": 6, "ff": 6}[stage]
            return trip * (8 * per) + 16 * ((ITEMS[stage] + n) // 2 + 1)

        def unit(stage, trip, n):
            per = {"heads": 6, "proj": 2, "window": 6, "merge": 4, "ff": 4}[stage]
            return trip * per + (UNITS[stage] + n)

        block = ctx.enter_context(nc.Block())

        @block.sync
        def _(sp):
            def load_item(stage, trip, n, src, kts=KT):
                sp.wait_ge(weights_ready, item(stage, trip, n) + 1)
                dst = raw[n % 2][:, 0:kts, :]
                sp.dma_start(dst, src).then_inc(raw_landed[n % 2], 16)

            for t in range(X_FIRST):
                sp.dma_start(x_in[t][:, :], x_tiles[t]).then_inc(x_landed[t], 16)
            sp.wait_ge(const_made, 5)
            for n in (A_UNITS - 2, A_UNITS - 1):
                sp.dma_start(window_proj[n, :, 0:PART], zeros[:, :]).then_inc(zeros_stored, 16)
            with sp.Fori(0, B_HEADS) as h:
                for n, col in enumerate((COL_QB, COL_KB, COL_VB, COL_CC, COL_CU, COL_CB)):
                    load_item("heads", h, n, w_in_k[:, :, bass.ds(h * PART + col, PART)])
            with sp.Fori(0, A_UNITS // 2) as t:
                for e in range(2):
                    load_item("proj", t, e, w_in_k[:, :, bass.ds(t * (2 * PART) + e * PART, PART)])

            with sp.Fori(0, TILES // 2) as t:
                for e in range(2):
                    m = t * (2 * PART) + e * PART
                    load_item("window", t, 3 * e, w_gate_k[:, :, bass.ds(m + WIDTH, PART)])
                    load_item("window", t, 3 * e + 1, w_gate_k[:, :, bass.ds(m + 2 * WIDTH, PART)])
                    load_item("window", t, 3 * e + 2, w_branch_k[:, BRANCH_KT:3 * BRANCH_KT, bass.ds(m, PART)])
                    sp.wait_ge(vector_done, V["heads"].end)
                    sp.wait_ge(tensor_done, T["heads"].end)
                    for n in range(2):
                        sp.wait_ge(proj_stored[n], 16 * (1 + A_UNITS // 2))
                    sp.wait_ge(zeros_stored, 32)
                    sp.wait_ge(tensor_done, T["window"].at(("scores", e, 1), t, back=1))
                    sp.dma_start(qf[e][:, :, :], window_proj[0:4, :, bass.ds(m + PART, PART)]
                                 .rearrange("j p t -> p j t")).then_inc(window_landed[e], 16)
                    for r in range(2):
                        sp.dma_start(kf[e][HEAD * r:HEAD * r + HEAD, :, :],
                                     window_proj[4, :, bass.ds(m + CHUNK, WINDOW)]
                                     .rearrange("(v p) t -> p v t", p=HEAD)).then_inc(window_landed[e], 16)
                    sp.dma_start(vf[e][:, :], window_proj[5, :, bass.ds(m, 2 * PART)])\
                      .then_inc(window_landed[e], 16)

            with sp.Fori(0, KT // 2) as t:
                for e in range(2):
                    m = t * (2 * PART) + e * PART
                    load_item("merge", t, 3 * e, w_gate_k[:, :, bass.ds(m, PART)])
                    load_item("merge", t, 3 * e + 1, w_branch_k[:, 0:BRANCH_KT, bass.ds(m, PART)], BRANCH_KT)
                    load_item("merge", t, 3 * e + 2, w_out_k[:, :, bass.ds(m, PART)])
                    sp.wait_ge(merged_stored, 16 * (1 + KT))
                    sp.wait_ge(vector_done, V["window"].end)
                    sp.wait_ge(scalar_done, S["window"].end)
                    sp.wait_ge(tensor_done, T["window"].end)
                    sp.wait_ge(vector_done, V["merge"].at(("acc", e, 1), t, back=1))
                    sp.dma_start(merged[:, :, bass.ds(m, PART)],
                                 merged_bc[bass.ds(t * 2 + e, 1), :, :].rearrange("o p (t c) -> p (o t) c", c=PART))\
                      .then_inc(merged_landed[e], 16)

            load_item("ff", 0, 0, w_ffn_k[:, :, 0:PART])
            load_item("ff", 0, 1, w_ffn_k[:, :, D_FF:D_FF + PART])
            sp.wait_ge(vector_done, V["merge"].end)
            sp.wait_ge(units_done, BUFFERS + UNITS["ff"])
            sp.dma_start(ln_gain[:, :], ln1_g[0:1, :].partition_broadcast(PART)).then_inc(ln_landed, 16)
            sp.dma_start(ln_shift[:, :], ln1_b[0:1, :].partition_broadcast(PART)).then_inc(ln_landed, 16)
            sp.dma_start(x_res[:, :], x_tiles[0]).then_inc(res_landed, 16)
            with sp.Fori(0, 3) as t:
                for e in range(2):
                    sp.wait_ge(vector_done, V["res"].at(("r1", e), t))
                    sp.dma_start(x_res[:, :], x_tiles[bass.ds(t * 2 + (e + 1), 1)].rearrange("o p d -> (o p) d"))\
                      .then_inc(res_landed, 16)
            sp.wait_ge(vector_done, V["res7"].at(("r1", 0)))
            sp.dma_start(x_res[:, :], x_tiles[TILES - 1]).then_inc(res_landed, 16)

            def ff_items(t, skip):
                c = t * (2 * PART)
                cols = (c, c + D_FF, c + PART, c + (D_FF + PART))
                for n, col in enumerate(cols):
                    if n >= skip:
                        load_item("ff", t, n, w_ffn_k[:, :, bass.ds(col, PART)])
                for s in range(2):
                    load_item("ff", t, 4 + s, w_down_k[bass.ds(t * 2 + s, 1)]
                              .rearrange("o p (k c) -> (o p) k c", c=PART))

            ff_items(0, 2)
            sp.wait_ge(tensor_done, T["res7"].end)
            sp.dma_start(ln2_gain[:, :], ln2_g[0:1, :].partition_broadcast(PART)).then_inc(ln2_landed, 16)
            sp.dma_start(ln2_shift[:, :], ln2_b[0:1, :].partition_broadcast(PART)).then_inc(ln2_landed, 16)
            with sp.Fori(1, FF_TRIPS) as t:
                ff_items(t, 0)
            for t in range(TILES):
                sp.wait_ge(vector_done, V["end"].at(("b", t)))
                sp.dma_start(out_tiles[t], y_acc[:, t, :]).then_inc(out_stored, 16)
            sp.wait_ge(out_stored, 16 * TILES)

        @block.gpsimd
        def _(pool):
            pool.memset(ident[:, :], 0.0).then_inc(const_made, 1)
            pool.wait_ge(const_made, 1)
            pool.affine_select(out=ident[:, :], in_=ident[:, :], compare_op=ALU.not_equal, fill=1.0, base=0,
                               pattern=[[-1, PART]], channel_multiplier=1).then_inc(const_made, 1)
            pool.memset(rms_eps[:, :], EPS * RMS_SHIFT).then_inc(const_made, 1)
            pool.memset(ln_eps[:, :], EPS).then_inc(const_made, 1)
            pool.memset(zeros[:, :], 0.0).then_inc(const_made, 1)
            pool.memset(proj_scale[:, 0:A_UNITS - 2], Q_SCALE).then_inc(const_made, 1)
            pool.memset(proj_scale[:, A_UNITS - 2:A_UNITS], 1.0).then_inc(const_made, 1)
            pool.iota(ramp_b[:, :], pattern=[[-1, TOKENS]], base=TOKENS - PART, channel_multiplier=1,
                      allow_small_or_imprecise_dtypes=True).then_inc(const_made, 1)
            pool.wait_ge(tensor_done, T["heads"].end)
            pool.wait_ge(vector_done, V["heads"].end)
            pool.wait_ge(scalar_done, S["heads"].end)
            pool.iota(ramp_a[:, :], pattern=[[-1, WINDOW]], base=CHUNK, channel_multiplier=1,
                      allow_small_or_imprecise_dtypes=True).then_inc(bias_a_made, 1)
            pool.wait_ge(bias_a_made, 1)
            pool.tensor_scalar(ramp_abs[:, :], ramp_a[:, :], -1.0, None, ALU.mult).then_inc(bias_a_made, 1)
            pool.wait_ge(bias_a_made, 2)
            pool.tensor_scalar(ramp_a[:, :], ramp_a[:, :], 0.0, None, ALU.max).then_inc(bias_a_made, 1)
            pool.wait_ge(bias_a_made, 3)
            pool.tensor_scalar(ramp_abs[:, :], ramp_abs[:, :], 0.0, None, ALU.max).then_inc(bias_a_made, 1)
            pool.wait_ge(bias_a_made, 4)
            pool.tensor_tensor(ramp_abs[:, :], ramp_abs[:, :], ramp_a[:, :], ALU.add).then_inc(bias_a_made, 1)
            pool.wait_ge(bias_a_made, 5)
            for h in range(A_HEADS):
                pool.tensor_scalar(bias_a[:, h, :], ramp_abs[:, :], 2.0 ** (-8.0 * (h + 1) / A_HEADS), None,
                                   ALU.mult).then_inc(bias_a_made, 1)
            pool.wait_ge(bias_a_made, 5 + A_HEADS)
            pool.tensor_copy(near_a[0:CHUNK, :, :], bias_a[0:CHUNK, :, 0:CHUNK]).then_inc(bias_a_made, 1)
            pool.wait_ge(bias_a_made, 6 + A_HEADS)
            pool.memset(bias_a[:, :, 0:CHUNK], MASKED).then_inc(bias_a_made, 1)
            pool.memset(bias_a[0:CHUNK, :, 2 * CHUNK:WINDOW], MASKED).then_inc(bias_a_made, 1)
            for g in range(2):
                pool.memset(a_prob[g][:, :, 0:CHUNK], 0.0).then_inc(bias_a_made, 1)
            pool.wait_ge(ln2_landed, 32)
            for t in range(TILES):
                pool.wait_ge(scalar_done, S["end"].at(("z", t)))
                pool.tensor_tensor(y_acc[:, t, :], y_acc[:, t, :], ln2_gain[:, :], ALU.mult).then_inc(gained, 1)

        @block.scalar
        def _(act):
            act.sem_inc(scalar_done, AHEAD)
            for n in range(2):
                act.sem_inc(proj_stored[n], 16)
            act.sem_inc(merged_stored, 16)

            def split_hi(stage, trip, n, dst, kts=KT, u=None):
                act.wait_ge(raw_landed[n % 2], landed(stage, trip, n))
                if u is not None:
                    act.wait_ge(units_done, u + 1)
                act.activation(dst, raw[n % 2][:, 0:kts, :], ACT.Copy).then_inc(weights_hi, 1)

            st = S["x"]
            for t in range(TILES):
                for hh in range(2):
                    act.wait_ge(tensor_done, T["x"].at(("x", t, hh)))
                    act.activation(act_h[:, 4 * hh:4 * hh + 4, PART * t:PART * t + PART],
                                   bank[2 * x_banks(t) + hh][:, :].rearrange("p (k c) -> p k c", c=PART),
                                   ACT.Copy).then_inc(scalar_done, st.step(("x", t, hh)))
                    if t == hh == 0:
                        for later in range(X_FIRST, TILES):
                            act.dma_start(x_in[later][:, :], x_tiles[later]).then_inc(x_landed[later], 16)
                        vectors = [(lam_in[:, n, :], v[0:1, :].partition_broadcast(PART))
                                   for n, v in enumerate((lam_q1, lam_k1, lam_q2, lam_k2))]
                        for dst, src in vectors:
                            act.dma_start(dst, src).then_inc(small_landed, 16)
                        act.dma_start(sink_in[:, :], sink[0:1, :].partition_broadcast(PART)).then_inc(small_landed, 16)
                        with nc.allow_non_contiguous_dma(reason="per-feature vectors, once"):
                            act.dma_start(gain_in[:, :], subln_g[0].rearrange("(p o) -> p o", o=1)).then_inc(small_landed, 16)
                            act.dma_start(gate_bias[:, :], b_gate[0].rearrange("(t p) -> p t", p=PART)).then_inc(small_landed, 16)
                            for c in range(C_TILES):
                                act.dma_start(conv_taps[:, c, :], conv_w[0].rearrange("w (c p) -> c p w", p=PART)[c])\
                                  .then_inc(small_landed, 16)
                if t == X_FIRST - 1:
                    split_hi("heads", 0, 0, w_h[0][:, :, :], u=unit("heads", 0, 0))
            st = S["init"]
            act.wait_ge(vector_done, V["init"].at("l1"))
            act.activation(lam_exp[:, :], lam_sum[:, :], ACT.Exp).then_inc(scalar_done, st.step("le"))

            st = S["heads"]
            with act.Fori(0, B_HEADS) as h:
                for s in HEADS:
                    k, a = s[0], s[1:]
                    if k == "split":
                        n = a[0]
                        split_hi("heads", h, n, w_h[n % 2][:, :, :], u=unit("heads", h, n))
                    elif k == "out":
                        n, half = a
                        cols = slice(HALF * half, HALF * half + HALF)
                        b = bank[2 * (n % 2) + half]
                        if n in (0, 1, 2, 3):
                            if half == 0:
                                act.wait_ge(tensor_done, T["heads"].at(("half", n), h))
                            else:
                                act.wait_ge(units_done, unit("heads", h, n) + 1 + BUFFERS)
                        if n in (0, 1):
                            act.wait_ge(tensor_done, T["heads"].at(("scores", 7, 1), h, back=1))
                            act.activation((q_h, k_h)[n][:, cols], b[:, :], ACT.Copy,
                                           scale=(Q_SCALE, 1.0)[n]).then_inc(scalar_done, st.step(s))
                        elif n == 2:
                            act.activation(v_t[:, cols], b[:, :], ACT.Copy).then_inc(scalar_done, st.step(s))
                        elif n == 3:
                            act.wait_ge(vector_done, V["heads"].at(("out", 5, 1), h, back=1))
                            act.activation(conv[:, cols], b[:, :], ACT.Copy).then_inc(scalar_done, st.step(s))
                        elif n == 5:
                            act.wait_ge(vector_done, V["heads"].at(("gate", half), h))
                            act.activation(yc_h[:, bass.ds(h, 1), cols].rearrange("p o c -> p (o c)"), conv[:, cols],
                                           ACT.Copy).then_inc(scalar_done, st.step(s))
                    elif k == "exps":
                        i = a[0]
                        keys = PART * (i + 1)
                        last = ("peak", i) if i >= 4 else ("logit", i, 0, 1)
                        act.wait_ge(vector_done, V["heads"].at(last, h))
                        for m in range(2):
                            act.activation(prob[i % 3][m][:, 0:keys], prob[i % 3][m][:, 0:keys], ACT.Exp, scale=-1.0,
                                           bias=low[:, i, m, 0:1], accum_out=den[:, i, m:m + 1])\
                               .then_inc(scalar_done, st.step(("exp", i, m)))
                    elif k == "turn":
                        i, g = a
                        n = min(4, i + 1 - 4 * g)
                        act.wait_ge(tensor_done, T["heads"].at(s, h))
                        act.activation(weights_t[:, 4 * g:4 * g + n, :],
                                       bank[TURN][:, 0:PART * n].rearrange("p (k c) -> p k c", c=PART),
                                       ACT.Copy).then_inc(scalar_done, st.step(s))
                    elif k == "vturn":
                        g = a[0]
                        act.wait_ge(tensor_done, T["heads"].at(s, h))
                        act.activation(v_b[:, 4 * g:4 * g + 4, :],
                                       bank[(TURN, VALUE)[g]][:, :].rearrange("p (k c) -> p k c", c=PART),
                                       ACT.Copy).then_inc(scalar_done, st.step(s))
                    elif k == "value":
                        i = a[0]
                        act.wait_ge(tensor_done, T["heads"].at(s, h))
                        values = bank[VALUE][:, PART * (i % 4):PART * (i % 4) + PART]
                        act.activation(mixed[:, i, :], values, ACT.Copy, scale=inv[:, i, 0:1])\
                           .then_inc(scalar_done, st.step(("out", "value", i)))
                        act.activation(squares[:, :], values, ACT.Square, scale=inv[:, i, 0:1],
                                       accum_out=square_sum[:, i:i + 1])\
                           .then_inc(scalar_done, st.step(("square", i)))
                    elif k == "rms":
                        act.wait_ge(scalar_done, st.at(("square", 7), h))
                        act.activation(rms_root[:, :], square_sum[:, :], ACT.Sqrt, scale=RMS_SHIFT / PART,
                                       bias=rms_eps[:, 0:1]).then_inc(scalar_done, st.step(("root",)))
                    elif k == "yturn":
                        g = a[0]
                        act.wait_ge(tensor_done, T["heads"].at(s, h))
                        act.activation(yb_h[:, bass.ds(h, 1), HALF * g:HALF * g + HALF].rearrange("p o c -> p (o c)"),
                                       bank[(TURN, VALUE)[g]][:, :], ACT.Copy, scale=rms_gain[:, 0:1])\
                           .then_inc(scalar_done, st.step(s))

            st = S["proj"]
            act.wait_ge(tensor_done, T["heads"].end)
            act.wait_ge(vector_done, V["heads"].at(("mix", 7), B_HEADS - 1))
            with act.Fori(0, A_UNITS // 2) as t:
                for e in range(2):
                    split_hi("proj", t, e + 1, w_h[(e + 1) % 2][:, :, :], u=unit("proj", t, e + 1))
                    act.wait_ge(proj_stored[e], t * 16 + 16)
                    for half in range(2):
                        if half == 0:
                            act.wait_ge(tensor_done, T["proj"].at(("half", e), t))
                        else:
                            act.wait_ge(units_done, unit("proj", t, e) + 1 + BUFFERS)
                        act.sem_inc(scales_seen, 1)
                        act.activation(to_dram[e][:, HALF * half:HALF * half + HALF], bank[2 * e + half][:, :],
                                       ACT.Copy, scale=proj_scale[:, bass.ds(t * 2 + e, 1)])\
                           .then_inc(scalar_done, st.step(("out", e, half)))
                    act.wait_ge(scalar_done, st.at(("out", e, 1), t))
                    act.dma_start(window_proj[bass.ds(t * 2 + e, 1), :, PART:PART + TOKENS]
                                  .rearrange("o p t -> (o p) t"), to_dram[e][:, :]).then_inc(proj_stored[e], 16)

            st = S["window"]
            act.wait_ge(bias_a_made, 10 + A_HEADS)
            with act.Fori(0, TILES // 2) as t:
                for s in WIN:
                    k, e, a = s[0], s[1], s[2:]
                    if k == "split":
                        n = e
                        split_hi("window", t, n, w_h[n % 2][:, :, :], u=unit("window", t, n))
                    elif k == "out" and a[0] < 2:
                        n, half = a
                        b = bank[2 * n + half]
                        if half == 0:
                            act.wait_ge(tensor_done, T["window"].at(("part", e, n, 24), t))
                        else:
                            act.wait_ge(units_done, unit("window", t, 3 * e + n) + 1 + BUFFERS)
                        if n == 0 and half == 0:
                            act.wait_ge(merged_stored, t * 32 + 16 * (e + 1))
                        act.sem_inc(gates_seen, 1)
                        act.activation((sig_b, sig_c)[n][:, HALF * half:HALF * half + HALF], b[:, :], ACT.Sigmoid,
                                       bias=gate_bias[:, bass.ds(t * 2 + (e + KT * (n + 1)), 1)])\
                           .then_inc(scalar_done, st.step(s))
                    elif k == "vturn":
                        act.wait_ge(tensor_done, T["window"].at(s, t))
                        act.activation(v_a[:, :, :, :],
                                       bank[TURN][:, 0:2 * PART].rearrange("p (b v c) -> p b v c", b=2, v=2),
                                       ACT.Copy).then_inc(scalar_done, st.step(s))
                    elif k == "scores":
                        g = a[0]
                        for n in range(A_GROUP):
                            act.wait_ge(vector_done, V["window"].at(("logit", e, g, n), t))
                            act.activation(a_prob[g][:, n, CHUNK:2 * PART], a_prob[g][:, n, CHUNK:2 * PART], ACT.Exp,
                                           scale=-1.0, bias=a_low[:, 4 * g + n:4 * g + n + 1],
                                           accum_out=a_den[:, 4 * g + n:4 * g + n + 1])\
                               .then_inc(scalar_done, st.step(("exp", e, g, n)))
                        act.wait_ge(vector_done, V["window"].at(("sub", e, g), t))
                        act.activation(a_sunk[:, 4 * g:4 * g + 4], a_sink[:, 4 * g:4 * g + 4], ACT.Exp)\
                           .then_inc(scalar_done, st.step(("sink", e, g)))
                    elif k == "turn":
                        act.wait_ge(tensor_done, T["window"].at(s, t))
                        act.activation(a_turned[a[1]][:, :, :], bank[TURN][:, :].rearrange("p (k c) -> p k c", c=PART),
                                       ACT.Copy).then_inc(scalar_done, st.step(s))
                    elif k == "yturn":
                        act.wait_ge(tensor_done, T["window"].at(s, t))
                        act.activation(ya_h[:, :, bass.ds(t * (2 * PART) + e * PART, PART)],
                                       bank[TURN][:, :].rearrange("p (k c) -> p k c", c=PART),
                                       ACT.Copy).then_inc(scalar_done, st.step(s))
                    elif k == "store":
                        act.wait_ge(vector_done, V["window"].at(("add", e), t))
                        act.dma_start(merged_bc[bass.ds(t * 2 + e, 1), :, :].rearrange("o p t -> (o p) t"),
                                      sig_b[:, :]).then_inc(merged_stored, 16)

            st = S["merge"]
            with act.Fori(0, KT // 2) as t:
                for e in range(2):
                    for n in range(2):
                        m = 3 * e + n + 1
                        if n == 0:
                            split_hi("merge", t, m, w_h[1][:, 0:BRANCH_KT, :], BRANCH_KT,
                                     u=unit("merge", t, 2 * e + 1))
                            for half in range(2):
                                if half == 0:
                                    act.wait_ge(tensor_done, T["merge"].at(("part", e, 0), t))
                                    act.wait_ge(vector_done, V["merge"].at(("acc", 1 - e, 1), t, back=1 - e))
                                else:
                                    act.wait_ge(units_done, unit("merge", t, 2 * e) + 1 + BUFFERS)
                                act.sem_inc(gates_seen, 1)
                                act.activation(sig_a[:, HALF * half:HALF * half + HALF], bank[half][:, :], ACT.Sigmoid,
                                               bias=gate_bias[:, bass.ds(t * 2 + e, 1)])\
                                   .then_inc(scalar_done, st.step(("out", e, half)))
                        else:
                            split_hi("merge", t, m, wo_h[:, :, bass.ds(t * (2 * PART) + e * PART, PART)])
                            split_hi("merge", t, m + 1, w_h[0][:, :, :], u=unit("merge", t, 2 * e + 2))

            def merged_hi(tile, g):
                act.activation(m_h[tile][:, 4 * g:4 * g + 4, :].rearrange("p k c -> p (k c)"),
                               merged[:, tile, HALF * g:HALF * g + HALF], ACT.Copy)\
                   .then_inc(scalar_done, S["res0"].step(("ms", tile, g)))

            act.wait_ge(vector_done, V["merge"].at(("acc", 1, 0), KT // 2 - 1))
            act.wait_ge(units_done, BUFFERS + UNITS["ff"])
            for tile in range(2):
                for g in range(2):
                    merged_hi(tile, g)

            def norm_scalar(stage, lab, trip, tile, slot):
                act.wait_ge(vector_done, V[stage].at(("ag", lab), trip))
                act.activation(ln_root[:, :], moments[:, 1:2], ACT.Sqrt, bias=ln_eps[:, 0:1])\
                   .then_inc(scalar_done, S[stage].step(("root", lab)))
                act.wait_ge(vector_done, V[stage].at(("b", lab), trip))
                act.activation(y_acc[:, bass.ds(tile, 1), :].rearrange("p o c -> p (o c)"), normed[slot][:, :], ACT.Copy,
                               scale=ALPHA).then_inc(scalar_done, S[stage].step(("keep", lab)))

            def norm_turned(stage, lab, trip, tile):
                for g in range(2):
                    act.wait_ge(tensor_done, T["ff_first" if lab == "t" else stage].at((f"turn{g}", lab), trip))
                    act.activation(act_h[:, 4 * g:4 * g + 4, bass.ds(tile * PART, PART)],
                                   bank[(TURN, VALUE)[g]][:, :].rearrange("p (k c) -> p k c", c=PART),
                                   ACT.Copy).then_inc(scalar_done, S[stage].step((f"turn{g}", lab)))

            with act.Fori(0, 3) as t:
                for e in range(2):
                    if e == 0:
                        act.wait_ge(tensor_done, T["res"].at(("m1", 1), t, back=1))
                        act.wait_ge(tensor_done, T["res0"].end)
                    else:
                        act.wait_ge(tensor_done, T["res"].at(("m1", 0), t))
                    act.activation(m_h[e][:, :, :].rearrange("p k c -> p (k c)"),
                                   merged[:, bass.ds(t * 2 + (e + 2), 1), :].rearrange("p o c -> p (o c)"),
                                   ACT.Copy).then_inc(scalar_done, S["res"].step(("ms", e)))
                    norm_scalar("res", e, t, t * 2 + e, e)
                    norm_turned("res", e, t, t * 2 + e)
            norm_scalar("res7", 0, 0, 6, 0)
            split_hi("ff", 0, 1, w_h[1][:, :, :], u=unit("ff", 0, 1))
            norm_turned("res7", 0, 0, 6)
            norm_scalar("res7", "t", 0, 7, 1)
            norm_turned("res7", "t", 0, 7)

            def ff(t):
                st = S["ff"]
                for s in range(2):
                    if s or not (isinstance(t, int) and t == 0):
                        split_hi("ff", t, 2 * s + 1, w_h[1][:, :, :], u=unit("ff", t, 2 * s + 1))
                    for half in range(2):
                        if half == 0:
                            act.wait_ge(tensor_done, in_ff(T, ("half", 2 * s), t))
                        else:
                            act.wait_ge(units_done, unit("ff", t, 2 * s) + 1 + BUFFERS)
                        act.wait_ge(vector_done, in_ff(V, ("lo", 1 - s, half), t, back=1 - s))
                        act.activation(silu[:, HALF * half:HALF * half + HALF], bank[half][:, :], ACT.Silu)\
                           .then_inc(scalar_done, st.step(("silu", s, half)))
                    if s == 0:
                        split_hi("ff", t, 2, w_h[0][:, :, :], u=unit("ff", t, 2))
                    else:
                        for d, slot in enumerate(down_slots(t)):
                            if d == 0 and slot == 0:
                                act.wait_ge(tensor_done, in_ff(T, ("down", TILES - 1, 1), t, back=1))
                            split_hi("ff", t, 4 + d, wd_h[slot][:, :].rearrange("p (k c) -> p k c", c=PART))
                        if not (isinstance(t, int) and t == FF_TRIPS - 1):
                            split_hi("ff", t, 6, w_h[0][:, :, :], u=unit("ff", t, 4))
                    for half in range(2):
                        act.wait_ge(vector_done, in_ff(V, ("up", s, half), t))
                        act.activation(h_h[down_slots(t)[s]][:, HALF * half:HALF * half + HALF],
                                       silu[:, HALF * half:HALF * half + HALF], ACT.Copy)\
                           .then_inc(scalar_done, st.step(("hi", s, half)))

            act.wait_ge(tensor_done, T["res7"].end)
            ff(0)
            with act.Fori(1, LOOPED) as t:
                ff(t)
            ff(LOOPED)
            ff(LOOPED + 1)
            for t in range(TILES):
                act.wait_ge(vector_done, V["end"].at(("ag", t)))
                act.activation(root2[:, t:t + 1], moments2[:, t, 1:2], ACT.Sqrt, bias=ln_eps[:, 0:1])\
                   .then_inc(scalar_done, S["end"].step(("root", t)))
                act.wait_ge(vector_done, V["end"].at(("off", t)))
                act.activation(y_acc[:, t, :], y_acc[:, t, :], ACT.Identity, scale=inv2[:, t:t + 1],
                               bias=offset2[:, t:t + 1]).then_inc(scalar_done, S["end"].step(("z", t)))

        @block.vector
        def _(dve):
            dve.sem_inc(vector_done, AHEAD)
            dve.sem_inc(weights_ready, BUFFERS)

            def f32(ap):
                return ap.bitcast(F32)

            def split_lo(stage, trip, n, hi, lo, kts=KT):
                dve.wait_ge(weights_hi, item(stage, trip, n) + 1)
                dve.tensor_tensor(lo, raw[n % 2][:, 0:kts, :], f32(hi), ALU.subtract).then_inc(weights_ready, 1)

            st = V["x"]
            for t in range(TILES):
                for hh in range(2):
                    cols = slice(PART * t, PART * t + PART)
                    dve.wait_ge(scalar_done, S["x"].at(("x", t, hh)))
                    dve.tensor_tensor(act_l[:, 4 * hh:4 * hh + 4, cols],
                                      bank[2 * x_banks(t) + hh][:, :].rearrange("p (k c) -> p k c", c=PART),
                                      f32(act_h[:, 4 * hh:4 * hh + 4, cols]), ALU.subtract)\
                       .then_inc(vector_done, st.step(("x", t, hh)))
                if t == X_FIRST - 1:
                    split_lo("heads", 0, 0, w_h[0][:, :, :], w_l[0][:, :, :])
            st = V["init"]
            dve.wait_ge(small_landed, 16 * (7 + C_TILES))
            for n in range(2):
                dve.tensor_tensor_reduce(out=lam_out[:, n, :], in0=lam_in[:, 2 * n, :], in1=lam_in[:, 2 * n + 1, :],
                                         scale=1.0, scalar=0.0, op0=ALU.mult, op1=ALU.add,
                                         accum_out=lam_sum[:, n:n + 1]).then_inc(vector_done, st.step(f"l{n}"))
            dve.wait_ge(scalar_done, S["init"].at("le"))
            dve.tensor_tensor(neg_lam[:, :], lam_exp[:, 0:1], lam_exp[:, 1:2], ALU.subtract)\
               .then_inc(vector_done, st.step("dl"))
            dve.wait_ge(vector_done, st.at("dl"))
            dve.tensor_scalar(neg_lam[:, :], neg_lam[:, :], LAMBDA_INIT, -1.0, ALU.add, ALU.mult)\
               .then_inc(vector_done, st.step("nl"))
            dve.tensor_scalar(rms_gain[:, :], gain_in[:, :], 1.0 - LAMBDA_INIT, None, ALU.mult)\
               .then_inc(vector_done, st.step("gain"))
            dve.tensor_scalar(neg_sink[:, :], sink_in[:, :], -1.0, None, ALU.mult)\
               .then_inc(vector_done, st.step("sink"))
            dve.wait_ge(const_made, 8)
            dve.scalar_tensor_tensor(out=bias_b[:, :], in0=ramp_b[:, :], scalar=-1.0, in1=ramp_b[:, :], op0=ALU.mult,
                                     op1=ALU.max).then_inc(vector_done, st.step("ramp"))
            dve.wait_ge(vector_done, st.at("ramp"))
            dve.memset(bias_b[0:CHUNK, TOKENS - CHUNK:TOKENS], MASKED).then_inc(const_made, 1)
            dve.memset(gated[:, 0:2], 0.0).then_inc(const_made, 1)

            st = V["heads"]
            dve.wait_ge(const_made, 10)
            dve.wait_ge(zeros_stored, 32)
            with dve.Fori(0, B_HEADS) as h:
                for s in HEADS:
                    k, a = s[0], s[1:]
                    if k == "split":
                        n = a[0]
                        split_lo("heads", h, n, w_h[n % 2][:, :, :], w_l[n % 2][:, :, :])
                    elif k == "decay":
                        dve.wait_ge(vector_done, st.at(("logit", 7, 1, 1), h, back=1))
                        dve.tensor_scalar(bias_b[:, :], bias_b[:, :], 2.0 ** (-8.0 / B_HEADS), None, ALU.mult)\
                           .then_inc(vector_done, st.step(s))
                    elif k == "out":
                        n, half = a
                        cols = slice(HALF * half, HALF * half + HALF)
                        b = bank[2 * (n % 2) + half]
                        if n in (0, 1):
                            dve.wait_ge(scalar_done, S["heads"].at(s, h))
                            if n == 0:
                                dve.scalar_tensor_tensor(out=q_l[:, cols], in0=b[:, :], scalar=Q_SCALE,
                                                         in1=f32(q_h[:, cols]), op0=ALU.mult, op1=ALU.subtract)\
                                   .then_inc(vector_done, st.step(s))
                            else:
                                dve.tensor_tensor(k_l[:, cols], b[:, :], f32(k_h[:, cols]), ALU.subtract)\
                                   .then_inc(vector_done, st.step(s))
                        elif n == 4:
                            dve.wait_ge(scalar_done, S["heads"].at(("out", 3, half), h))
                            if half == 0:
                                dve.wait_ge(tensor_done, T["heads"].at(("half", 4), h))
                                dve.wait_ge(vector_done, st.at(("conv", 2), h, back=1))
                            else:
                                dve.wait_ge(units_done, unit("heads", h, 4) + 1 + BUFFERS)
                            dve.tensor_tensor(gated[:, 2 + HALF * half:2 + HALF * half + HALF], b[:, :], conv[:, cols],
                                              ALU.mult).then_inc(vector_done, st.step(s))
                        elif n == 5:
                            if half == 0:
                                dve.wait_ge(tensor_done, T["heads"].at(("half", 5), h))
                                dve.wait_ge(vector_done, st.at(("conv", 2), h))
                            else:
                                dve.wait_ge(units_done, unit("heads", h, 5) + 1 + BUFFERS)
                            dve.tensor_tensor(conv[:, cols], b[:, :], conv[:, cols], ALU.mult)\
                               .then_inc(vector_done, st.step(("gate", half)))
                            dve.wait_ge(scalar_done, S["heads"].at(s, h))
                            tile = bass.ds(h, 1)
                            dve.tensor_tensor(yc_l[:, tile, cols].rearrange("p o c -> p (o c)"), conv[:, cols],
                                              f32(yc_h[:, tile, cols].rearrange("p o c -> p (o c)")), ALU.subtract)\
                               .then_inc(vector_done, st.step(s))
                    elif k == "conv":
                        tap = [conv_taps[:, bass.ds(h, 1), w:w + 1].rearrange("p o w -> p (o w)") for w in range(3)]
                        dve.wait_ge(vector_done, st.at(("out", 4, 1), h))
                        dve.tensor_scalar(conv[:, :], gated[:, 0:TOKENS], tap[0], None, ALU.mult)\
                           .then_inc(vector_done, st.step(("conv", 0)))
                        for w in (1, 2):
                            dve.wait_ge(vector_done, st.at(("conv", w - 1), h))
                            dve.scalar_tensor_tensor(out=conv[:, :], in0=gated[:, w:w + TOKENS], scalar=tap[w],
                                                     in1=conv[:, :], op0=ALU.mult, op1=ALU.add)\
                               .then_inc(vector_done, st.step(("conv", w)))
                    elif k == "scores":
                        i, c = a
                        keys = min(HALF, PART * (i + 1) - HALF * c)
                        off = PART * (7 - i) + HALF * c
                        dve.wait_ge(tensor_done, T["heads"].at(s, h))
                        dve.sem_inc(scores_seen, 1)
                        for m in range(2):
                            dve.tensor_tensor_reduce(out=prob[i % 3][m][:, HALF * c:HALF * c + keys],
                                                     in0=bank[SCORES[m]][:, 0:keys], in1=bias_b[:, off:off + keys],
                                                     scale=1.0, scalar=3e38, op0=ALU.add, op1=ALU.min,
                                                     accum_out=low[:, i, m, c:c + 1])\
                               .then_inc(vector_done, st.step(("logit", i, c, m)))
                        if c == 1:
                            dve.wait_ge(vector_done, st.at(("logit", i, 1, 1), h))
                            dve.tensor_tensor(low[:, i, :, 0], low[:, i, :, 0], low[:, i, :, 1], ALU.min)\
                               .then_inc(vector_done, st.step(("peak", i)))
                    elif k == "mix":
                        i = a[0]
                        p, keys = prob[i % 3], PART * (i + 1)
                        dve.wait_ge(scalar_done, S["heads"].at(("exp", i, 1), h))
                        dve.reciprocal(inv[:, i, :], den[:, i, :]).then_inc(vector_done, st.step(("inv", i)))
                        dve.wait_ge(vector_done, st.at(("inv", i), h))
                        dve.scalar_tensor_tensor(out=coef[:, i:i + 1], in0=den[:, i, 0:1], scalar=inv[:, i, 1:2],
                                                 in1=neg_lam[:, :], op0=ALU.mult, op1=ALU.mult)\
                           .then_inc(vector_done, st.step(("coef", i)))
                        dve.wait_ge(vector_done, st.at(("coef", i), h))
                        dve.scalar_tensor_tensor(out=p[0][:, 0:keys], in0=p[1][:, 0:keys], scalar=coef[:, i:i + 1],
                                                 in1=p[0][:, 0:keys], op0=ALU.mult, op1=ALU.add)\
                           .then_inc(vector_done, st.step(("mix", i)))
                    elif k == "rms":
                        dve.wait_ge(scalar_done, S["heads"].at(("root",), h))
                        dve.reciprocal(rms_inv[:, :], rms_root[:, :]).then_inc(vector_done, st.step(("rinv",)))
                        dve.wait_ge(vector_done, st.at(("rinv",), h))
                        dve.tensor_scalar(rms_inv[:, :], rms_inv[:, :], RMS_SHIFT ** 0.5, None, ALU.mult)\
                           .then_inc(vector_done, st.step(("rscale",)))
                        dve.wait_ge(vector_done, st.at(("rscale",), h))
                        dve.tensor_tensor(mixed[:, :, :], mixed[:, :, :],
                                          rms_inv[:, :].rearrange("p (t o) -> p t o", o=1)
                                          .to_broadcast([PART, TILES, PART]), ALU.mult)\
                           .then_inc(vector_done, st.step(("rmul",)))
                    elif k == "yturn":
                        g = a[0]
                        tile = bass.ds(h, 1)
                        dve.wait_ge(scalar_done, S["heads"].at(s, h))
                        cols = slice(HALF * g, HALF * g + HALF)
                        dve.scalar_tensor_tensor(out=yb_l[:, tile, cols].rearrange("p o c -> p (o c)"),
                                                 in0=bank[(TURN, VALUE)[g]][:, :], scalar=rms_gain[:, 0:1],
                                                 in1=f32(yb_h[:, tile, cols].rearrange("p o c -> p (o c)")),
                                                 op0=ALU.mult, op1=ALU.subtract).then_inc(vector_done, st.step(s))

            with dve.Fori(0, A_UNITS // 2) as t:
                for e in range(2):
                    split_lo("proj", t, e + 1, w_h[(e + 1) % 2][:, :, :], w_l[(e + 1) % 2][:, :, :])

            st = V["window"]
            dve.wait_ge(bias_a_made, 10 + A_HEADS)
            with dve.Fori(0, TILES // 2) as t:
                for s in WIN:
                    k, e, a = s[0], s[1], s[2:]
                    if k == "split":
                        n = e
                        split_lo("window", t, n, w_h[n % 2][:, :, :], w_l[n % 2][:, :, :])
                    elif k == "out" and a[0] == 2:
                        q = a[1]
                        br, half = divmod(q, 2)
                        if q < 3:
                            dve.wait_ge(tensor_done, T["window"].at(("part", e, 2, 12 * (q + 1)), t))
                        else:
                            dve.wait_ge(units_done, unit("window", t, 3 * e + 2) + 1 + BUFFERS)
                        cols = slice(HALF * half, HALF * half + HALF)
                        sig = (sig_b, sig_c)[br]
                        dve.wait_ge(scalar_done, S["window"].at(("out", e, br, half), t))
                        dve.tensor_tensor(sig[:, cols], bank[2 * br + half][:, :], sig[:, cols], ALU.mult)\
                           .then_inc(vector_done, st.step(s))
                    elif k == "scores":
                        g = a[0]
                        dve.wait_ge(tensor_done, T["window"].at(s, t))
                        dve.sem_inc(scores_seen, 1)
                        for n in range(A_GROUP):
                            hd = A_GROUP * g + n
                            dve.tensor_tensor_reduce(out=a_prob[g][:, n, CHUNK:2 * PART],
                                                     in0=bank[SCORES[n % 2]][:, WINDOW * (n // 2):WINDOW * (n // 2) + WINDOW],
                                                     in1=bias_a[:, hd, :], scale=1.0, scalar=neg_sink[:, hd:hd + 1],
                                                     op0=ALU.add, op1=ALU.min, accum_out=a_low[:, hd:hd + 1])\
                               .then_inc(vector_done, st.step(("logit", e, g, n)))
                        dve.wait_ge(vector_done, st.at(("logit", e, g, 3), t))
                        dve.tensor_tensor(a_sink[:, 4 * g:4 * g + 4], a_low[:, 4 * g:4 * g + 4],
                                          neg_sink[:, 4 * g:4 * g + 4], ALU.subtract)\
                           .then_inc(vector_done, st.step(("sub", e, g)))
                    elif k == "norm":
                        dve.wait_ge(scalar_done, S["window"].at(("sink", e, 1), t))
                        dve.tensor_tensor(a_inv[:, :], a_den[:, :], a_sunk[:, :], ALU.add)\
                           .then_inc(vector_done, st.step(("den", e)))
                        dve.wait_ge(vector_done, st.at(("den", e), t))
                        dve.reciprocal(a_inv[:, :], a_inv[:, :]).then_inc(vector_done, st.step(("inv", e)))
                        dve.wait_ge(vector_done, st.at(("inv", e), t))
                        dve.wait_ge(tensor_done, T["window"].at(("value", e, 1, 1), t))
                        dve.sem_inc(scores_seen, 1)
                        dve.tensor_tensor(a_mix[:, :, :], bank[VALUE][:, :].rearrange("p (n c) -> p n c", c=HEAD),
                                          a_inv[:, :].rearrange("p (t o) -> p t o", o=1)
                                          .to_broadcast([PART, A_HEADS, HEAD]), ALU.mult)\
                           .then_inc(vector_done, st.step(("norm", e)))
                    elif k == "yturn":
                        cols = bass.ds(t * (2 * PART) + e * PART, PART)
                        dve.wait_ge(scalar_done, S["window"].at(s, t))
                        dve.tensor_tensor(ya_l[:, :, cols], bank[TURN][:, :].rearrange("p (k c) -> p k c", c=PART),
                                          f32(ya_h[:, :, cols]), ALU.subtract).then_inc(vector_done, st.step(s))
                    elif k == "unmask":
                        dve.wait_ge(vector_done, st.at(("logit", e, 1, 3), t))
                        dve.tensor_copy(bias_a[0:CHUNK, :, 0:CHUNK], near_a[0:CHUNK, :, :])\
                           .then_inc(vector_done, st.step(s))
                    elif k == "add":
                        dve.wait_ge(vector_done, st.at(("out", e, 2, 3), t))
                        dve.tensor_tensor(sig_b[:, :], sig_b[:, :], sig_c[:, :], ALU.add)\
                           .then_inc(vector_done, st.step(s))

            st = V["merge"]
            with dve.Fori(0, KT // 2) as t:
                for e in range(2):
                    split_lo("merge", t, 3 * e + 1, w_h[1][:, 0:BRANCH_KT, :], w_l[1][:, 0:BRANCH_KT, :], BRANCH_KT)
                    m = bass.ds(t * (2 * PART) + e * PART, PART)
                    split_lo("merge", t, 3 * e + 2, wo_h[:, :, m], wo_l[:, :, m])
                    split_lo("merge", t, 3 * e + 3, w_h[0][:, :, :], w_l[0][:, :, :])
                    for half in range(2):
                        if half == 0:
                            dve.wait_ge(tensor_done, T["merge"].at(("part", e, 1), t))
                            dve.wait_ge(merged_landed[e], t * 16 + 16)
                        else:
                            dve.wait_ge(units_done, unit("merge", t, 2 * e + 1) + 1 + BUFFERS)
                        cols = slice(HALF * half, HALF * half + HALF)
                        dve.wait_ge(scalar_done, S["merge"].at(("out", e, half), t))
                        dve.tensor_tensor(sig_a[:, cols], bank[2 + half][:, :], sig_a[:, cols], ALU.mult)\
                           .then_inc(vector_done, st.step(("mul", e, half)))
                        dve.wait_ge(vector_done, st.at(("mul", e, half), t))
                        part = merged[:, 4 * half:4 * half + 4, m]
                        dve.tensor_tensor(part, part, sig_a[:, cols].rearrange("p (t c) -> p t c", c=PART), ALU.add)\
                           .then_inc(vector_done, st.step(("acc", e, half)))

            def merged_lo(stage, label, e, tile, trip=0):
                dve.wait_ge(scalar_done, S[stage].at(label, trip))
                dve.tensor_tensor(m_l[e][:, :, :].rearrange("p k c -> p (k c)"), tile,
                                  f32(m_h[e][:, :, :].rearrange("p k c -> p (k c)")), ALU.subtract)\
                   .then_inc(vector_done, V[stage].step(label))

            for tile in range(2):
                for g in range(2):
                    part = slice(4 * g, 4 * g + 4)
                    dve.wait_ge(scalar_done, S["res0"].at(("ms", tile, g)))
                    dve.tensor_tensor(m_l[tile][:, part, :].rearrange("p k c -> p (k c)"),
                                      merged[:, tile, HALF * g:HALF * g + HALF],
                                      f32(m_h[tile][:, part, :].rearrange("p k c -> p (k c)")), ALU.subtract)\
                       .then_inc(vector_done, V["res0"].step(("ms", tile, g)))
            dve.wait_ge(ln_landed, 32)

            def layer_norm(stage, lab, trip, y, gain, shift):
                st = V[stage]
                for half in range(2):
                    dve.bn_stats(stats[:, half, :], y[:, HALF * half:HALF * half + HALF])\
                       .then_inc(vector_done, st.step((f"st{half}", lab)))
                dve.wait_ge(vector_done, st.at(("st1", lab), trip))
                dve.sem_inc(moments_seen, 1)
                dve.bn_aggr(moments[:, :], stats[:, :, :].rearrange("p a b -> p (a b)"))\
                   .then_inc(vector_done, st.step(("ag", lab)))
                dve.wait_ge(scalar_done, S[stage].at(("root", lab), trip))
                dve.reciprocal(ln_inv[:, :], ln_root[:, :]).then_inc(vector_done, st.step(("ri", lab)))
                dve.wait_ge(vector_done, st.at(("ri", lab), trip))
                dve.tensor_scalar(y, y, moments[:, 0:1], ln_inv[:, 0:1], ALU.subtract, ALU.mult)\
                   .then_inc(vector_done, st.step(("z", lab)))
                dve.wait_ge(vector_done, st.at(("z", lab), trip))
                dve.tensor_tensor(y, y, gain[:, :], ALU.mult).then_inc(vector_done, st.step(("g", lab)))
                dve.wait_ge(vector_done, st.at(("g", lab), trip))
                dve.tensor_tensor(y, y, shift[:, :], ALU.add).then_inc(vector_done, st.step(("b", lab)))

            def residual(stage, lab, trip, slot, landed_at, done0, done1):
                for half, done in enumerate((done0, done1)):
                    cols = slice(HALF * half, HALF * half + HALF)
                    if half == 0:
                        dve.wait_ge(res_landed, landed_at)
                    for d in done:
                        dve.wait_ge(tensor_done, d)
                    dve.scalar_tensor_tensor(out=normed[slot][:, cols], in0=x_res[:, cols], scalar=ALPHA,
                                             in1=bank[2 * slot + half][:, :], op0=ALU.mult, op1=ALU.add)\
                       .then_inc(vector_done, V[stage].step((f"r{half}", lab)))
                dve.wait_ge(vector_done, V[stage].at(("r1", lab), trip))

            def norm(stage, lab, trip, slot):
                layer_norm(stage, lab, trip, normed[slot][:, :], ln_gain, ln_shift)

            def turned_lo(stage, lab, trip, tile):
                for g in range(2):
                    cols = bass.ds(tile * PART, PART)
                    dve.wait_ge(scalar_done, S[stage].at((f"turn{g}", lab), trip))
                    dve.tensor_tensor(act_l[:, 4 * g:4 * g + 4, cols],
                                      bank[(TURN, VALUE)[g]][:, :].rearrange("p (k c) -> p k c", c=PART),
                                      f32(act_h[:, 4 * g:4 * g + 4, cols]), ALU.subtract)\
                       .then_inc(vector_done, V[stage].step((f"turn{g}", lab)))

            with dve.Fori(0, 3) as t:
                for e in range(2):
                    if e == 0:
                        done = [(T["res"].at((f"m{n}", 1), t, back=1), T["res0"].at(f"m{n}")) for n in range(2)]
                    else:
                        done = [(T["res"].at((f"m{n}", 0), t),) for n in range(2)]
                    residual("res", e, t, e, t * 32 + 16 * (e + 1), *done)
                    merged_lo("res", ("ms", e), e, merged[:, bass.ds(t * 2 + (e + 2), 1), :]
                              .rearrange("p o c -> p (o c)"), t)
                    norm("res", e, t, e)
                    turned_lo("res", e, t, t * 2 + e)
            residual("res7", 0, 0, 0, 16 * 7, (T["res"].at(("m0", 1), 2),), (T["res"].at(("m1", 1), 2),))
            norm("res7", 0, 0, 0)
            split_lo("ff", 0, 1, w_h[1][:, :, :], w_l[1][:, :, :])
            turned_lo("res7", 0, 0, 6)
            residual("res7", "t", 0, 1, 16 * 8, (T["res7"].at(("m0", 0)),), (T["res7"].at(("m1", 0)),))
            norm("res7", "t", 0, 1)
            turned_lo("res7", "t", 0, 7)

            def ff(t):
                st = of(V, t)[0]
                for s in range(2):
                    slots = down_slots(t)
                    if s or not (isinstance(t, int) and t == 0):
                        split_lo("ff", t, 2 * s + 1, w_h[1][:, :, :], w_l[1][:, :, :])
                    if s == 0:
                        split_lo("ff", t, 2, w_h[0][:, :, :], w_l[0][:, :, :])
                    else:
                        for d, slot in enumerate(slots):
                            split_lo("ff", t, 4 + d, wd_h[slot][:, :].rearrange("p (k c) -> p k c", c=PART),
                                     wd_l[slot][:, :].rearrange("p (k c) -> p k c", c=PART))
                        if not (isinstance(t, int) and t == FF_TRIPS - 1):
                            split_lo("ff", t, 6, w_h[0][:, :, :], w_l[0][:, :, :])
                    for half in range(2):
                        cols = slice(HALF * half, HALF * half + HALF)
                        dve.wait_ge(scalar_done, S["ff"].at(("silu", s, half), t))
                        if half == 0:
                            dve.wait_ge(tensor_done, in_ff(T, ("half", 2 * s + 1), t))
                        else:
                            dve.wait_ge(units_done, unit("ff", t, 2 * s + 1) + 1 + BUFFERS)
                        dve.tensor_tensor(silu[:, cols], bank[2 + half][:, :], silu[:, cols], ALU.mult)\
                           .then_inc(vector_done, st.step(("up", s, half)))
                        dve.wait_ge(scalar_done, S["ff"].at(("hi", s, half), t))
                        dve.tensor_tensor(h_l[slots[s]][:, cols], silu[:, cols], f32(h_h[slots[s]][:, cols]),
                                          ALU.subtract).then_inc(vector_done, st.step(("lo", s, half)))

            def add_down(t, st, tile):
                for half in range(2):
                    part = y_acc[:, tile, HALF * half:HALF * half + HALF]
                    b = bank[(4, 0)[tile // 2 % 2] + 2 * (tile % 2) + half]
                    dve.wait_ge(tensor_done, in_ff(T, ("down", tile, half), t))
                    dve.tensor_tensor(part, b[:, :], part, ALU.add)\
                       .then_inc(vector_done, st.step(("acc", tile, half)))

            ff(0)
            for tile in range(TILES):
                add_down(0, V["ff"], tile)
            with dve.Fori(1, LOOPED) as t:
                ff(t)
                for tile in range(TILES):
                    add_down(t, V["ff"], tile)
            ff(LOOPED)
            ff(LOOPED + 1)
            st = V["end"]
            dve.wait_ge(ln2_landed, 32)
            for t in range(TILES + 2):
                if t < TILES:
                    add_down(FF_TRIPS - 1, st, t)
                    dve.wait_ge(vector_done, st.at(("acc", t, 1)))
                    for half in range(2):
                        dve.bn_stats(stats[:, half, :], y_acc[:, t, HALF * half:HALF * half + HALF])\
                           .then_inc(vector_done, st.step((f"st{half}", t)))
                    dve.wait_ge(vector_done, st.at(("st1", t)))
                    dve.bn_aggr(moments2[:, t, :], stats[:, :, :].rearrange("p a b -> p (a b)"))\
                       .then_inc(vector_done, st.step(("ag", t)))
                    dve.wait_ge(scalar_done, S["end"].at(("root", t)))
                    dve.reciprocal(inv2[:, t:t + 1], root2[:, t:t + 1]).then_inc(vector_done, st.step(("ri", t)))
                    dve.wait_ge(vector_done, st.at(("ri", t)))
                    dve.scalar_tensor_tensor(out=offset2[:, t:t + 1], in0=moments2[:, t, 0:1], scalar=-1.0,
                                             in1=inv2[:, t:t + 1], op0=ALU.mult, op1=ALU.mult)\
                       .then_inc(vector_done, st.step(("off", t)))
                if t >= 2:
                    dve.wait_ge(gained, t - 1)
                    dve.tensor_tensor(y_acc[:, t - 2, :], y_acc[:, t - 2, :], ln2_shift[:, :], ALU.add)\
                       .then_inc(vector_done, st.step(("b", t - 2)))

        @block.tensor
        def _(pe):
            pe.sem_inc(tensor_done, AHEAD)
            pe.sem_inc(units_done, BUFFERS)

            def three(out_ap, stat, mov, start, stop):
                pairs = ((stat[0], mov[0]), (stat[0], mov[1]), (stat[1], mov[0]))
                for n, (lhs, rhs) in enumerate(pairs):
                    ins = pe.matmul(out_ap, lhs, rhs, start=start and n == 0, stop=stop and n == 2)
                return ins

            def one(b, slot, k, half, n, a_h, a_l, start, stop, row=None):
                row = k if row is None else row
                cols = slice(HALF * half, HALF * half + HALF)
                lhs = (w_h[slot], w_h[slot], w_l[slot])[n][:, k, :]
                rhs = (a_h, a_l, a_h)[n][:, row, cols]
                return pe.matmul(b[:, :], lhs, rhs, start=start, stop=stop)

            def turn(b, blocks):
                for n, src in enumerate(blocks):
                    ins = pe.transpose(b[:, PART * n:PART * n + PART], src, ident[:, :])
                return ins

            st = T["x"]
            pe.wait_ge(const_made, 2)
            for t in range(TILES):
                pe.wait_ge(x_landed[t], 16)
                for hh in range(2):
                    if t >= 4:
                        pe.wait_ge(vector_done, V["x"].at(("x", t - 3, hh)))
                    turn(bank[2 * x_banks(t) + hh], [x_in[t][:, PART * k:PART * k + PART]
                                                  for k in range(4 * hh, 4 * hh + 4)])\
                        .then_inc(tensor_done, st.step(("x", t, hh)))

            st = T["heads"]
            vd = V["heads"]
            with pe.Fori(0, B_HEADS) as h:
                for s in HEADS:
                    k, a = s[0], s[1:]
                    if k == "mm":
                        n, lo, hi = a
                        for idx in range(lo, hi):
                            half, r = divmod(idx, 24)
                            kt, p = divmod(r, 3)
                            b = bank[2 * (n % 2) + half]
                            if idx == 0:
                                pe.wait_ge(weights_ready, item("heads", h, n) + 1 + BUFFERS)
                            if r == 0:
                                if n == 0:
                                    pe.wait_ge(vector_done, vd.at(("out", 4, half), h, back=1))
                                    pe.wait_ge(vector_done, V["x"].at(("x", 4 * half + 3, 1)))
                                elif n == 1:
                                    pe.wait_ge(vector_done, vd.at(("gate", half), h, back=1))
                                elif n in (2, 3):
                                    pe.wait_ge(vector_done, vd.at(("out", n - 2, half), h))
                                else:
                                    pe.wait_ge(scalar_done, S["heads"].at(("out", n - 2, half), h))
                            ins = one(b, n % 2, kt, half, p, act_h, act_l, r == 0, r == 23)
                            if idx == 23:
                                ins.then_inc(tensor_done, st.step(("half", n)))
                            elif idx == 47:
                                ins.then_inc(units_done, 1)
                    elif k == "scores":
                        i, c = a
                        keys = max(2 * PART, min(HALF, PART * (i + 1) - HALF * c))
                        if i == 0:
                            pe.wait_ge(vector_done, vd.at(("out", 1, 1), h))
                        else:
                            before = (i, 0) if c else (i - 1, int(i - 1 >= 4))
                            pe.wait_ge(vector_done, vd.at(("logit", *before, 1), h))
                        for p in range(3):
                            for m in range(2):
                                rows = slice(HEAD * m, HEAD * m + HEAD)
                                q = (q_h, q_h, q_l)[p][rows, PART * i:PART * i + PART]
                                kk = (k_h, k_l, k_h)[p][rows, HALF * c:HALF * c + keys]
                                ins = pe.matmul(bank[SCORES[m]][:, 0:keys], q, kk, start=p == 0, stop=p == 2)
                        ins.then_inc(tensor_done, st.step(s))
                    elif k == "turn":
                        i, g = a
                        n = min(4, i + 1 - 4 * g)
                        if g == 0:
                            pe.wait_ge(vector_done, vd.at(("mix", i), h))
                        before = (("turn", i, 0) if g else
                                  ("vturn", 0) if i == 0 else ("turn", i - 1, int(i - 1 >= 4)))
                        pe.wait_ge(scalar_done, S["heads"].at(before, h))
                        turn(bank[TURN], [prob[i % 3][0][:, PART * j:PART * j + PART]
                                          for j in range(4 * g, 4 * g + n)]).then_inc(tensor_done, st.step(s))
                    elif k == "vturn":
                        g = a[0]
                        pe.wait_ge(scalar_done, S["heads"].at(("out", 2, g), h))
                        pe.wait_ge(vector_done, vd.at(("yturn", g), h, back=1))
                        turn(bank[(TURN, VALUE)[g]], [v_t[:, PART * j:PART * j + PART]
                                                      for j in range(4 * g, 4 * g + 4)])\
                            .then_inc(tensor_done, st.step(s))
                    elif k == "value":
                        i = a[0]
                        pe.wait_ge(scalar_done, S["heads"].at(("turn", i, int(i >= 4)), h))
                        pe.wait_ge(scalar_done, S["heads"].at(("square", i - 4) if i >= 4 else ("vturn", 1), h))
                        for j in range(i + 1):
                            ins = pe.matmul(bank[VALUE][:, PART * (i % 4):PART * (i % 4) + PART], weights_t[:, j, :],
                                            v_b[:, j, :], start=j == 0, stop=j == i)
                        ins.then_inc(tensor_done, st.step(s))
                    elif k == "yturn":
                        g = a[0]
                        if g == 0:
                            pe.wait_ge(vector_done, vd.at(("rmul",), h))
                        turn(bank[(TURN, VALUE)[g]], [mixed[:, j, :] for j in range(4 * g, 4 * g + 4)])\
                            .then_inc(tensor_done, st.step(s))

            st = T["proj"]
            with pe.Fori(0, A_UNITS // 2) as t:
                for e in range(2):
                    pe.wait_ge(weights_ready, item("proj", t, e) + 1 + BUFFERS)
                    for half in range(2):
                        pe.wait_ge(scalar_done, S["proj"].at(("out", e, half), t, back=1))
                        pe.wait_ge(vector_done, V["heads"].at(("gate", half) if e else ("out", 4, half), B_HEADS - 1))
                        for idx in range(24):
                            kt, p = divmod(idx, 3)
                            ins = one(bank[2 * e + half], e, kt, half, p, act_h, act_l, idx == 0, idx == 23)
                        if half == 0:
                            ins.then_inc(tensor_done, st.step(("half", e)))
                        else:
                            ins.then_inc(units_done, 1)

            st = T["window"]
            vd = V["window"]
            with pe.Fori(0, TILES // 2) as t:
                for s in WIN:
                    k, e, a = s[0], s[1], s[2:]
                    if k == "mm":
                        n, lo, hi = a
                        per = 24 if n < 2 else 12
                        for idx in range(lo, hi):
                            q, r = divmod(idx, per)
                            kt, p = divmod(r, 3)
                            br, half = (n, q) if n < 2 else divmod(q, 2)
                            if idx == 0:
                                pe.wait_ge(weights_ready, item("window", t, 3 * e + n) + 1 + BUFFERS)
                            if r == 0:
                                if n < 2:
                                    pe.wait_ge(vector_done, vd.at(("out", 1 - e, 2, 2 * n + half), t, back=1 - e))
                                    pe.wait_ge(scalar_done, S["proj"].at(("out", n, half), A_UNITS // 2 - 1))
                                else:
                                    pe.wait_ge(scalar_done, S["window"].at(("out", e, br, half), t))
                            b = bank[2 * br + half]
                            slot = (3 * e + n) % 2
                            if n < 2:
                                ins = one(b, slot, kt, half, p, act_h, act_l, r == 0, r == per - 1)
                            else:
                                y = ((yb_h, yb_l), (yc_h, yc_l))[br]
                                ins = one(b, slot, BRANCH_KT * br + kt, half, p, *y, r == 0, r == per - 1, row=kt)
                            if idx == 47:
                                ins.then_inc(units_done, 1)
                            elif r == per - 1:
                                ins.then_inc(tensor_done, st.step(("part", e, n, idx + 1)))
                    elif k == "vturn":
                        pe.wait_ge(window_landed[e], t * 64 + 64)
                        pe.wait_ge(vector_done, vd.at(("yturn", 1 - e), t, back=1 - e))
                        turn(bank[TURN], [vf[e][:, 0:PART], vf[e][:, PART:2 * PART]]).then_inc(tensor_done, st.step(s))
                    elif k == "scores":
                        g = a[0]
                        pe.wait_ge(vector_done, vd.at(("logit", e, 0, 3), t) if g else
                                   vd.at(("logit", 1 - e, 1, 3), t, back=1 - e))
                        for pair in range(2):
                            for r in range(2):
                                rows = slice(HEAD * r, HEAD * r + HEAD)
                                ins = pe.matmul(bank[SCORES[r]][:, WINDOW * pair:WINDOW * pair + WINDOW],
                                                qf[e][rows, 2 * g + pair, :], kf[e][rows, g, :], start=True, stop=True)
                        ins.then_inc(tensor_done, st.step(s))
                    elif k == "turn":
                        g, pair = a
                        pe.wait_ge(scalar_done, S["window"].at(("exp", e, g, 2 * pair + 1), t))
                        before = ("turn", e, g, 0) if pair else ("turn", e, 0, 1) if g else ("vturn", e)
                        pe.wait_ge(scalar_done, S["window"].at(before, t))
                        turn(bank[TURN], [a_prob[g][:, 2 * pair + n, PART * blk:PART * blk + PART]
                                          for n in range(2) for blk in range(2)]).then_inc(tensor_done, st.step(s))
                    elif k == "value":
                        g, pair = a
                        pe.wait_ge(scalar_done, S["window"].at(("turn", e, g, pair), t))
                        if g == pair == 0:
                            pe.wait_ge(vector_done, vd.at(("norm", 1 - e), t, back=1 - e))
                        for n in range(2):
                            c = HEAD * (4 * g + 2 * pair + n)
                            for blk in range(2):
                                ins = pe.matmul(bank[VALUE][:, c:c + HEAD], a_turned[pair][:, 2 * n + blk, :],
                                                v_a[:, blk, g, :], start=blk == 0, stop=blk == 1)
                        ins.then_inc(tensor_done, st.step(s))
                    elif k == "yturn":
                        pe.wait_ge(vector_done, vd.at(("norm", e), t))
                        pe.wait_ge(scalar_done, S["window"].at(("turn", e, 1, 1), t))
                        turn(bank[TURN], [a_mix[:, 2 * n:2 * n + 2, :].rearrange("p a c -> p (a c)")
                                          for n in range(4)]).then_inc(tensor_done, st.step(s))

            st = T["merge"]
            with pe.Fori(0, KT // 2) as t:
                for e in range(2):
                    for n in range(2):
                        kts = (KT, BRANCH_KT)[n]
                        pe.wait_ge(weights_ready, item("merge", t, 3 * e + n) + 1 + BUFFERS)
                        for half in range(2):
                            if n == 0:
                                pe.wait_ge(scalar_done, S["merge"].at(("out", 1 - e, half), t, back=1 - e))
                            else:
                                pe.wait_ge(vector_done, V["merge"].at(("mul", 1 - e, half), t, back=1 - e))
                            pe.wait_ge(vector_done, V["window"].at(("out", 1, 2, 2 * n + half), TILES // 2 - 1))
                            for idx in range(3 * kts):
                                kt, p = divmod(idx, 3)
                                a_h, a_l = ((act_h, act_l), (ya_h, ya_l))[n]
                                ins = one(bank[2 * n + half], n, kt, half, p, a_h, a_l, idx == 0, idx == 3 * kts - 1)
                            if half == 0:
                                ins.then_inc(tensor_done, st.step(("part", e, n)))
                            else:
                                ins.then_inc(units_done, 1)

            def project(slot, stage, labels):
                for half in range(2):
                    cols = slice(HALF * half, HALF * half + HALF)
                    for kt in range(KT):
                        if stage == "res0" and kt in (0, 4):
                            pe.wait_ge(vector_done, V["res0"].at(("ms", 0, kt // 4)))
                        ins = three(bank[2 * slot + half][:, :], (m_h[slot][:, kt, :], m_l[slot][:, kt, :]),
                                    (wo_h[:, kt, cols], wo_l[:, kt, cols]), kt == 0, kt == KT - 1)
                    ins.then_inc(tensor_done, T[stage].step(labels[half]))

            def turn_normed(stage, lab, trip, slot, before):
                pe.wait_ge(vector_done, V[stage].at(("b", lab), trip))
                for g in range(2):
                    pe.wait_ge(vector_done, before[g])
                    turn(bank[(TURN, VALUE)[g]], [normed[slot][:, PART * k:PART * k + PART]
                                                  for k in range(4 * g, 4 * g + 4)])\
                        .then_inc(tensor_done, T["ff_first" if lab == "t" else stage].step((f"turn{g}", lab)))

            pe.wait_ge(weights_ready, item("merge", KT // 2, 0) + BUFFERS)
            project(0, "res0", ("m0", "m1"))
            with pe.Fori(0, 3) as t:
                for e in range(2):
                    slot = 1 - e
                    if e == 0:
                        pe.wait_ge(vector_done, V["res"].at(("ms", 1), t, back=1))
                        pe.wait_ge(vector_done, V["res0"].at(("ms", 1, 1)))
                    else:
                        pe.wait_ge(vector_done, V["res"].at(("ms", 0), t))
                    project(slot, "res", (("m0", e), ("m1", e)))
                    turn_normed("res", e, t, e, [V["res"].at((f"turn{g}", 1 - e), t, back=1 - e) for g in range(2)])
            pe.wait_ge(vector_done, V["res"].at(("ms", 1), 2))
            project(1, "res7", (("m0", 0), ("m1", 0)))
            turn_normed("res7", 0, 0, 0, [V["res"].at((f"turn{g}", 1), 2) for g in range(2)])

            def unit_half(t, n, half, lo=0, hi=24):
                if half == lo == 0:
                    pe.wait_ge(weights_ready, item("ff", t, n) + 1 + BUFFERS)
                for idx in range(lo, hi):
                    kt, p = divmod(idx, 3)
                    ins = one(bank[2 * (n % 2) + half], n % 2, kt, half, p, act_h, act_l, idx == 0, idx == 23)
                if hi == 24 and half == 0:
                    ins.then_inc(tensor_done, of(T, t)[0].step(("half", n)))
                elif hi == 24:
                    ins.then_inc(units_done, 1)

            def bank_taken(t, n, half):
                if n == 2:
                    pe.wait_ge(scalar_done, S["ff"].at(("silu", 0, half), t))
                elif n == 3:
                    pe.wait_ge(vector_done, in_ff(V, ("up", 0, half), t))
                elif not (isinstance(t, int) and t == LOOPED + 1):
                    pe.wait_ge(vector_done, in_ff(V, ("acc", 6 + n, half), t, back=1))
                elif n == 0:
                    pe.wait_ge(scalar_done, S["ff"].at(("silu", 1, half), t - 1))
                else:
                    pe.wait_ge(vector_done, in_ff(V, ("up", 1, half), t, back=1))

            def units(t, first):
                for n in range(first, 4):
                    for half in range(2):
                        bank_taken(t, n, half)
                        unit_half(t, n, half)

            def down(t, slots):
                st = of(T, t)[0]
                pe.wait_ge(weights_ready, item("ff", t, 5) + 1 + BUFFERS)
                for quad in range(TILES // 2):
                    places = [(s, 2 * quad + n, half) for s in slots for n in range(2) for half in range(2)]
                    if len(slots) == 4 and quad:
                        places.sort(key=lambda p: p[1:])
                    for s, tile, half in places:
                        b = bank[(4, 0)[quad % 2] + 2 * (tile % 2) + half]
                        if quad == 0 and s in (slots[0], slots[-1]):
                            pe.wait_ge(vector_done, in_ff(V, ("lo", int(s == slots[-1]), 1), t))
                        if s == slots[0]:
                            if quad == 0 and len(slots) == 4:
                                pe.wait_ge(vector_done, V["ff"].at(("acc", 4 + tile, half), LOOPED - 1))
                            elif quad == 0:
                                pe.wait_ge(vector_done, in_ff(V, ("acc", 4 + tile, half), t, back=1))
                            elif quad == 1:
                                pe.wait_ge(vector_done, in_ff(V, ("up", 1, half), t))
                                pe.wait_ge(scalar_done, S["ff"].at(("silu", 1, half), t))
                            elif len(slots) == 4:
                                pe.wait_ge(vector_done, V["end"].at(("acc", tile - 4, half)))
                            else:
                                pe.wait_ge(vector_done, in_ff(V, ("acc", tile - 4, half), t))
                        rows = slice(PART * tile, PART * tile + PART)
                        cols = slice(HALF * half, HALF * half + HALF)
                        ins = three(b[:, :], (h_h[s][:, rows], h_l[s][:, rows]),
                                    (wd_h[s][:, cols], wd_l[s][:, cols]), s == slots[0], s == slots[-1])
                        if s == slots[-1]:
                            ins.then_inc(tensor_done, st.step(("down", tile, half)))

            pe.wait_ge(vector_done, V["res7"].at(("r1", 0)))
            unit_half(0, 0, 0)
            pe.wait_ge(vector_done, V["res7"].at(("r0", "t")))
            unit_half(0, 1, 0, 0, 15)
            turn_normed("res7", "t", 0, 1, [V["res7"].at((f"turn{g}", 0)) for g in range(2)])
            unit_half(0, 1, 0, 15, 24)
            pe.wait_ge(vector_done, V["res7"].end)
            unit_half(0, 0, 1)
            unit_half(0, 1, 1)
            units(0, 2)
            down(0, (0, 1))
            with pe.Fori(1, LOOPED) as t:
                units(t, 0)
                down(t, (0, 1))
            units(LOOPED, 0)
            units(LOOPED + 1, 0)
            down(LOOPED + 1, (0, 1, 2, 3))


_INS = ["x", "w_in", "sink", "lam_q1", "lam_k1", "lam_q2", "lam_k2", "subln_g", "conv_w", "w_branch", "w_gate", "b_gate",
        "w_out", "ln1_g", "ln1_b", "w_ffn_in", "w_ffn_down", "ln2_g", "ln2_b"]


def kernel(**inputs):
    import numpy as np
    import concourse.bacc as bacc
    from concourse.bass_utils import run_bass_kernel_spmd

    nc = bacc.Bacc("TRN2", target_bir_lowering=False, num_devices=1, dynamic_dma_scratch_size=1024)
    arrays, args = {}, []
    for name in _INS:
        a = np.ascontiguousarray(inputs[name])
        arrays[f"in_{name}"] = a
        args.append(nc.dram_tensor(f"in_{name}", a.shape, mybir.dt.from_np(a.dtype), kind="ExternalInput").ap())
    shape = inputs["x"].shape
    args.append(nc.dram_tensor("out_dram", shape, F32, kind="ExternalOutput").ap())
    hybrid_encoder_layer(nc, *args)
    r = run_bass_kernel_spmd(nc, [arrays], core_ids=[0])
    return r.results[0]["out_dram"]
```
